# Optimizing a Trainium2 kernel written in Bass

```python
import jax, jax.numpy as jnp
from jax import lax
import numpy as np

D_MODEL = 1024
BATCH = 1
SEQ = 512
DEPTH = 1

CHUNK = 64
P_DIM = 256
G_WIDTH = 1024
G_GROUPS = 8
G_GROUP_DIM = G_WIDTH // G_GROUPS
G_BLOCK = 128
M_HEADS = 4
M_QK_DIM = 128
M_V_DIM = 256
M_QK = M_HEADS * M_QK_DIM
M_V = M_HEADS * M_V_DIM
M_CHUNK = CHUNK
FORGET_BIAS = 3.0
N_EXPERTS = 64
TOP_K = 8
N_GROUPS = 8
TOPK_GROUPS = 4
D_EXPERT = 256
D_SHARED = 256
ROUTE_SCALE = 2.5
MOE_POS_BLOCK = 128
ALPHA = (2 * DEPTH) ** 0.25
BETA = (8 * DEPTH) ** -0.25
LN_EPS = 1e-5
RMS_EPS = 1e-6
D_IN = 2 * G_WIDTH + 2 * M_QK + 2 * M_V + 2 * M_HEADS + 2 * D_MODEL
SPLIT_POINTS = (
    G_WIDTH,
    2 * G_WIDTH,
    2 * G_WIDTH + M_QK,
    2 * G_WIDTH + 2 * M_QK,
    2 * G_WIDTH + 2 * M_QK + M_V,
    2 * G_WIDTH + 2 * M_QK + 2 * M_V,
    2 * G_WIDTH + 2 * M_QK + 2 * M_V + M_HEADS,
    2 * G_WIDTH + 2 * M_QK + 2 * M_V + 2 * M_HEADS,
    2 * G_WIDTH + 2 * M_QK + 2 * M_V + 2 * M_HEADS + D_MODEL,
)
F_OFF = 2 * G_WIDTH + 2 * M_QK + 2 * M_V + M_HEADS

kernel_name = "hybrid_gmlp_mlstm_moe_deepnorm"

def layer_norm(x, g, b):
    xf = x.astype(jnp.float32)
    mu = jnp.mean(xf, -1, keepdims=True)
    var = jnp.mean(jnp.square(xf - mu), -1, keepdims=True)
    return ((xf - mu) * lax.rsqrt(var + LN_EPS) * g + b).astype(x.dtype)

def spatial_gating(u, v, ln_g, ln_b, w_s, b_s):
    B, S, _ = v.shape
    v = layer_norm(v, ln_g, ln_b)
    v = v.reshape(B, S // G_BLOCK, G_BLOCK, G_GROUPS, G_GROUP_DIM)
    pos = jnp.arange(G_BLOCK)
    mask = (pos[None, :] // CHUNK) <= (pos[:, None] // CHUNK)
    w = jnp.where(mask[None], w_s, jnp.zeros((), w_s.dtype))
    mixed = jnp.einsum('gts,bnsgc->bntgc', w, v) + b_s.T[None, None, :, :, None]
    return u * mixed.reshape(B, S, G_WIDTH)

def mlstm_chunkwise(q, k, v, i_pre, f_pre):
    B, S, H, _ = q.shape
    L = M_CHUNK
    NC = S // L

    def to_chunks(t):
        t = t.reshape((B, NC, L, H) + t.shape[3:])
        return jnp.moveaxis(t, (1, 3), (0, 2))

    q = q * (M_QK_DIM ** -0.5)
    lf = jax.nn.log_sigmoid(f_pre)
    xs = (to_chunks(q), to_chunks(k), to_chunks(v), to_chunks(i_pre), to_chunks(lf))
    tri = jnp.tril(jnp.ones((L, L), dtype=bool))

    def step(carry, inp):
        C, n, m = carry
        qb, kb, vb, li, lfb = inp
        b = jnp.cumsum(lfb, axis=-1)
        d = b[..., :, None] - b[..., None, :] + li[..., None, :]
        d = jnp.where(tri, d, -jnp.inf)
        inter = b + m[..., None]
        m_t = jnp.maximum(inter, jnp.max(d, -1))
        w_intra = jnp.exp(d - m_t[..., None])
        w_inter = jnp.exp(inter - m_t)
        s = jnp.einsum('bhtd,bhsd->bhts', qb, kb) * w_intra
        num = (jnp.einsum('bhts,bhsv->bhtv', s, vb)
               + w_inter[..., None] * jnp.einsum('bhtd,bhdv->bhtv', qb, C))
        den = jnp.sum(s, -1) + w_inter * jnp.einsum('bhtd,bhd->bht', qb, n)
        h = num / jnp.maximum(jnp.abs(den), jnp.exp(-m_t))[..., None]
        b_last = b[..., -1]
        g = b_last[..., None] - b + li
        m_new = jnp.maximum(b_last + m, jnp.max(g, -1))
        decay = jnp.exp(b_last + m - m_new)
        wk = jnp.exp(g - m_new[..., None])[..., None] * kb
        C = decay[..., None, None] * C + jnp.einsum('bhsd,bhsv->bhdv', wk, vb)
        n = decay[..., None] * n + jnp.sum(wk, -2)
        return (C, n, m_new), h

    init = (jnp.zeros((B, H, M_QK_DIM, M_V_DIM), jnp.float32),
            jnp.zeros((B, H, M_QK_DIM), jnp.float32),
            jnp.zeros((B, H), jnp.float32))
    _, h = lax.scan(step, init, xs)
    return jnp.moveaxis(h, (0, 2), (1, 3)).reshape(B, S, H, M_V_DIM)

def token_mixer(x, w_in, b_in, sg_ln_g, sg_ln_b, w_s, b_s, mh_g, w_pa, w_pb, w_out):
    B, S, _ = x.shape
    f32 = jnp.float32
    z = jnp.einsum('bsd,de->bse', x, w_in) + b_in
    u, v, q, k, vm, o, ig, fg, ga, gb = jnp.split(z, SPLIT_POINTS, axis=-1)
    a = spatial_gating(jax.nn.gelu(u, approximate=False), jax.nn.gelu(v, approximate=False),
                       sg_ln_g, sg_ln_b, w_s, b_s)
    h = mlstm_chunkwise(q.reshape(B, S, M_HEADS, M_QK_DIM).astype(f32),
                        k.reshape(B, S, M_HEADS, M_QK_DIM).astype(f32),
                        vm.reshape(B, S, M_HEADS, M_V_DIM).astype(f32),
                        ig.astype(f32), fg.astype(f32))
    h = h * lax.rsqrt(jnp.mean(h * h, -1, keepdims=True) + RMS_EPS)
    mb = (jax.nn.sigmoid(o.astype(f32)) * (h.reshape(B, S, M_V) * mh_g)).astype(x.dtype)
    y = jax.nn.sigmoid(ga) * (a @ w_pa) + jax.nn.sigmoid(gb) * (mb @ w_pb)
    return y @ w_out

def moe(x, w_router, b_router, w_gate_e, w_up_e, w_down_e, w_gate_s, w_up_s, w_down_s):
    B, S, D = x.shape
    nblk = S // MOE_POS_BLOCK
    T = B * MOE_POS_BLOCK
    xt = x.reshape(B, nblk, MOE_POS_BLOCK, D).transpose(1, 0, 2, 3).reshape(nblk, T, D)
    per_group = N_EXPERTS // N_GROUPS

    def block(xb):
        scores = jax.nn.sigmoid(jnp.einsum('td,de->te', xb, w_router).astype(jnp.float32))
        sel = scores + b_router.astype(jnp.float32)
        grp_score = jnp.sum(lax.top_k(sel.reshape(T, N_GROUPS, per_group), 2)[0], -1)
        _, gidx = lax.top_k(grp_score, TOPK_GROUPS)
        gmask = jnp.any(gidx[..., None] == jnp.arange(N_GROUPS), axis=-2)
        emask = jnp.repeat(gmask, per_group, axis=-1)
        _, eidx = lax.top_k(jnp.where(emask, sel, -jnp.inf), TOP_K)
        wsel = jnp.take_along_axis(scores, eidx, -1)
        wsel = wsel / jnp.sum(wsel, -1, keepdims=True) * ROUTE_SCALE
        combine = jnp.zeros((T, N_EXPERTS), jnp.float32).at[jnp.arange(T)[:, None], eidx].set(wsel)
        hg = jnp.einsum('td,edf->tef', xb, w_gate_e)
        hu = jnp.einsum('td,edf->tef', xb, w_up_e)
        hid = jax.nn.silu(hg) * hu * combine[..., None].astype(xb.dtype)
        routed = jnp.einsum('tef,efd->td', hid, w_down_e)
        shared = (jax.nn.silu(xb @ w_gate_s) * (xb @ w_up_s)) @ w_down_s
        return routed + shared

    out = lax.map(block, xt)
    return out.reshape(nblk, B, MOE_POS_BLOCK, D).transpose(1, 0, 2, 3).reshape(B, S, D)

def setup_inputs(seed: int = 0) -> dict:
    key = jax.random.key(seed)
    ks = jax.random.split(key, 32)
    L = DEPTH

    def nrm(k, shape, scale):
        return jax.random.normal(k, shape, jnp.float32) * scale

    forget_off = jnp.zeros((D_IN,), jnp.float32).at[F_OFF:F_OFF + M_HEADS].set(FORGET_BIAS)
    return {
        "x": nrm(ks[0], (BATCH, SEQ, D_MODEL), 1.0),
        "p": nrm(ks[1], (DEPTH, BATCH, SEQ, P_DIM), 1.0),
        "w_in": nrm(ks[2], (L, D_MODEL, D_IN), D_MODEL ** -0.5),
        "b_in": nrm(ks[3], (L, D_IN), 0.02) + forget_off,
        "sg_ln_g": 1.0 + nrm(ks[4], (L, G_WIDTH), 0.02),
        "sg_ln_b": nrm(ks[5], (L, G_WIDTH), 0.02),
        "w_s": nrm(ks[6], (L, G_GROUPS, G_BLOCK, G_BLOCK), G_BLOCK ** -0.5),
        "b_s": 1.0 + nrm(ks[7], (L, G_GROUPS, G_BLOCK), 0.02),
        "mh_g": 1.0 + nrm(ks[8], (L, M_V), 0.02),
        "w_pa": nrm(ks[9], (L, G_WIDTH, D_MODEL), G_WIDTH ** -0.5 * BETA),
        "w_pb": nrm(ks[10], (L, M_V, D_MODEL), M_V ** -0.5 * BETA),
        "w_out": nrm(ks[11], (L, D_MODEL, D_MODEL), D_MODEL ** -0.5 * BETA),
        "ln1_g": 1.0 + nrm(ks[12], (L, D_MODEL), 0.02),
        "ln1_b": nrm(ks[13], (L, D_MODEL), 0.02),
        "w_router": nrm(ks[14], (L, D_MODEL, N_EXPERTS), D_MODEL ** -0.5),
        "b_router": nrm(ks[15], (L, N_EXPERTS), 0.01),
        "w_gate_e": nrm(ks[16], (L, N_EXPERTS, D_MODEL, D_EXPERT), D_MODEL ** -0.5),
        "w_up_e": nrm(ks[17], (L, N_EXPERTS, D_MODEL, D_EXPERT), D_MODEL ** -0.5),
        "w_down_e": nrm(ks[18], (L, N_EXPERTS, D_EXPERT, D_MODEL), D_EXPERT ** -0.5 * BETA),
        "w_gate_s": nrm(ks[19], (L, D_MODEL, D_SHARED), D_MODEL ** -0.5),
        "w_up_s": nrm(ks[20], (L, D_MODEL, D_SHARED), D_MODEL ** -0.5),
        "w_down_s": nrm(ks[21], (L, D_SHARED, D_MODEL), D_SHARED ** -0.5 * BETA),
        "w_pg": nrm(ks[22], (L, D_MODEL, D_MODEL), D_MODEL ** -0.5),
        "b_pg": nrm(ks[23], (L, D_MODEL), 0.02),
        "w_p": nrm(ks[24], (L, P_DIM, D_MODEL), P_DIM ** -0.5 * BETA),
        "ln2_g": 1.0 + nrm(ks[25], (L, D_MODEL), 0.02),
        "ln2_b": nrm(ks[26], (L, D_MODEL), 0.02),
    }

def reference(x, p, w_in, b_in, sg_ln_g, sg_ln_b, w_s, b_s, mh_g, w_pa, w_pb, w_out,
              ln1_g, ln1_b, w_router, b_router, w_gate_e, w_up_e, w_down_e,
              w_gate_s, w_up_s, w_down_s, w_pg, b_pg, w_p, ln2_g, ln2_b):
    for l in range(DEPTH):
        mix = token_mixer(x, w_in[l], b_in[l], sg_ln_g[l], sg_ln_b[l], w_s[l], b_s[l],
                          mh_g[l], w_pa[l], w_pb[l], w_out[l])
        x = layer_norm(ALPHA * x + mix, ln1_g[l], ln1_b[l])
        ffn = moe(x, w_router[l], b_router[l], w_gate_e[l], w_up_e[l], w_down_e[l],
                  w_gate_s[l], w_up_s[l], w_down_s[l])
        ple = jax.nn.sigmoid(x @ w_pg[l] + b_pg[l]) * (p[l] @ w_p[l])
        x = layer_norm(ALPHA * x + ffn + ple, ln2_g[l], ln2_b[l])
    return x


_drawn_inputs = setup_inputs


def setup_inputs(seed=0):
    import zlib

    import numpy as np

    out = dict(_drawn_inputs(seed))
    spreads = {}
    factors = {'sg_ln_g': 10.388,
     'sg_ln_b': 12.123,
     'b_s': 10.994,
     'mh_g': 14.156,
     'b_pg': 30.723,
     'ln2_g': 21.998,
     'ln2_b': 21.987}
    for name, (base, spread) in spreads.items():
        noise = np.random.default_rng([zlib.crc32(name.encode()), seed]).standard_normal(out[name].shape)
        drawn = base * np.exp(spread * noise) if base else spread * noise
        out[name] = __import__('jax').numpy.asarray(drawn.astype(out[name].dtype))
    for name, factor in factors.items():
        out[name] = (out[name] * factor).astype(out[name].dtype)
    return out
```

```python
import concourse.bass as bass
from concourse import mybir
from contextlib import ExitStack
import math

F32 = mybir.dt.float32
F32R = mybir.dt.float32r
I32 = mybir.dt.int32
U32 = mybir.dt.uint32
ALU = mybir.AluOpType
ACT = mybir.ActivationFunctionType
AX = mybir.AxisListType

P = 128
D = 1024
SEQ = 512
NT = SEQ // P
NK = D // P
CHUNK = 64
NC = SEQ // CHUNK
GW, GG = 1024, 8
MH, QK, MV = 4, 128, 256
MVE = MV + 1
NEXP, TOPK, NGRP, TOPG = 64, 8, 8, 4
DE = 256
ROUTE_SCALE = 2.5
DEPTH = 1
ALPHA = (2 * DEPTH) ** 0.25
LN_EPS, RMS_EPS = 1e-5, 1e-6
BIG_NEG = -1.0e30

C_U, C_V = 0, GW
C_Q = 2 * GW
C_K = C_Q + MH * QK
C_VM = C_K + MH * QK
C_O = C_VM + MH * MV
C_I = C_O + MH * MV
C_F = C_I + MH
C_GA = C_F + MH
C_GB = C_GA + D
W = 512
HK = NK // 2


class Count:

    def __init__(self, eng, sem):
        self.eng, self.sem, self.base, self.more = eng, sem, 0, 0

    def inc(self, ins):
        ins.then_inc(self.sem, 1)
        self.more += 1
        return ins

    def link(self, ins):
        self.inc(ins)
        self.eng.wait_ge(self.sem, self.base + self.more)

    def enter(self, i, per):
        self.total, self.per, self.more = self.base + self.more, per, 0
        self.base = self.total + i * per

    def leave(self, n):
        assert self.more == self.per, (self.more, self.per)
        self.base, self.more = self.total + n * self.per, 0


def wait_any(eng, s, value):
    if not (isinstance(value, int) and value == 0):
        eng.wait_ge(s, value)


def experts_in_order(eng, expert, n):
    for u in range(4):
        expert(u, u, 0)
    with eng.Fori(1, n // 4) as i:
        for j in range(4):
            expert(4 * i + j, j, i)


def build(nc, A, out):
    ctx = ExitStack()
    with ctx:
        def sem(name):
            return ctx.enter_context(nc.semaphore(name))

        ARENA = -(-nc.sbuf_base // 64) * 64

        def sb(name, shape, dt, at):
            return nc.alloc_sbuf_tensor_at(name, shape, dt, offset=ARENA + at)

        KB = 1024
        at_xh, at_xl, at_raw, at_hi, at_lo = 0, 16 * KB, 32 * KB, 48 * KB, 64 * KB
        at_r1, at_r2, at_r3, at_r4, at_r5 = 80 * KB, 96 * KB, 112 * KB, 128 * KB, 144 * KB
        at_small = at_r5 + 4 * NT * MH * MVE
        xT_h = sb("xT_h", [P, NK, SEQ], F32R, at_xh)
        xT_l = sb("xT_l", [P, NK, SEQ], F32R, at_xl)
        yT_h = sb("yT_h", [P, NK, SEQ], F32R, at_xh)
        yT_l = sb("yT_l", [P, NK, SEQ], F32R, at_xl)
        raw = [sb(f"raw{s}", [P, HK, W], F32, at_raw + 8 * KB * s) for s in range(2)]
        w_h = [sb(f"w_h{s}", [P, HK, W], F32R, at_hi + 8 * KB * s) for s in range(2)]
        w_l = [sb(f"w_l{s}", [P, HK, W], F32R, at_lo + 8 * KB * s) for s in range(2)]
        qkT = sb("qkT", [P, 2, MH, SEQ], F32, at_r1)
        osig = sb("osig", [P, NT, D], F32, at_r1)
        xres = sb("xres", [P, NT, D], F32, at_r1)
        x_in = sb("x_in", [P, NT, D], F32, at_r2)
        v_sb = sb("v_sb", [P, NT, GW], F32, at_r2)
        aT_h = sb("aT_h", [P, NK, SEQ], F32R, at_r2)
        mT_h = sb("mT_h", [P, NK, SEQ], F32R, at_r2)
        x1T_h = sb("x1T_h", [P, NK, SEQ], F32R, at_r2)
        ws_in = sb("ws_in", [P, GG, P], F32, at_r3)
        aT_l = sb("aT_l", [P, NK, SEQ], F32R, at_r3)
        mT_l = sb("mT_l", [P, NK, SEQ], F32R, at_r3)
        x1T_l = sb("x1T_l", [P, NK, SEQ], F32R, at_r3)
        row = [sb(f"row{n}", [MH, SEQ], F32, at_r4 + 2 * KB * n) for n in range(8)]
        r_f, r_t, r_a, r_b, r_cm, r_one, r_neg, r_em = row
        uT = sb("uT", [P, NK, SEQ], F32, at_r4)
        yT = sb("yT", [P, NK, SEQ], F32, at_r4)
        vme = sb("vme", [P, NT, MH, MVE], F32, at_r5)
        gbT = sb("gbT", [P, NK, SEQ], F32, at_r5)

        spot = [at_small]

        def small(name, shape, dt=F32):
            size = 4 * math.prod(shape[1:])
            t = sb(name, shape, dt, spot[0])
            spot[0] += -(-size // 32) * 32
            return t

        ident = small("ident", [P, P])
        ones = small("ones", [P, P])
        intra = small("intra", [P, P])
        sel = small("sel", [MH, MH, P])
        mark = small("mark", [P, 4])
        eps_ln = small("eps_ln", [P, 1])
        bias_bc = [small(f"bias_bc{n}", [P, D]) for n in range(2)]
        at_ws = spot[0]
        wsT = small("wsT", [P, GG, P])
        add_bc = small("add_bc", [P, GG, P])
        at_state = spot[0]
        state = small("state", [P, NC, MVE])
        wg_h = sb("wg_h", [P, NK, P], F32R, at_state)
        wg_l = sb("wg_l", [P, NK, P], F32R, at_state + 4 * KB)
        kw = small("kw", [P, NT, P])
        q_pad = small("q_pad", [P, NT, 2, P])
        wS = small("wS", [P, NT, P])
        wexp = small("wexp", [P, NT, P])
        tmp = small("tmp", [P, W])
        wg_raw = sb("wg_raw", [P, NK, P], F32, at_r3 + 4 * KB)
        u_row = small("u_row", [MH, SEQ])
        win_row = small("win_row", [MH, SEQ])
        cols = small("cols", [P, NT, 3 * MH])
        dec_row = small("dec_row", [MH, NC])
        dec_bc = small("dec_bc", [P, MH, NC])
        m_row = small("m_row", [MH, NC + 1])
        g_row = small("g_row", [MH, NC])
        bif = small("bif", [MH, 2])
        NROW = 7 * NK
        vec = sb("vec", [NROW, P], F32, at_r3 + 8 * KB)
        bcol = small("bcol", [P, NROW])
        B_QK, B_U, B_GA, B_GB, B_SG, B_SB, B_MG = range(0, NROW, NK)
        stat = small("stat", [P, NT, 2, 6])
        mv = small("mv", [P, NT, 2])
        rstd = small("rstd", [P, NT])
        eps_rms = small("eps_rms", [P, 1])
        den = small("den", [P, NT, MH])
        ssq = small("ssq", [P, NT, MH])
        hsc = small("hsc", [P, NT, MH])
        hs2 = small("hs2", [P, NT, MH])
        junk = small("junk", [P, MV])
        x1_rows = nc.dram_tensor("x1_rows", [SEQ, D], F32).ap()
        y_rows = nc.dram_tensor("y_rows", [SEQ * TOPK, D], F32).ap()
        gu = [sb(f"gu{j}", [P, NK, 2 * DE], F32, at) for j, at in
              enumerate((at_r5, at_raw, at_hi, at_lo))]
        dn = [sb(f"dn{j}", [P, 2, D], F32, at) for j, at in
              enumerate((at_r4, at_r4 + 8 * KB, 0, 8 * KB))]
        xg = [sb(f"xg{n}", [P, D], F32, (16 + 4 * n) * KB) for n in range(2)]
        xgT = [sb(f"xgT{n}", [P, NK, P], F32, (24 + 4 * n) * KB) for n in range(2)]
        spot2 = [at_small + 8 * P]

        def small2(name, shape, dt=F32):
            size = 4 * math.prod(shape[1:])
            t = sb(name, shape, dt, spot2[0])
            spot2[0] += -(-size // 32) * 32
            return t

        assert spot2[0] <= at_small + 2 * 4 * P
        NU = NEXP + 2
        before = small2("before", [P, P])
        spot2[0] = at_ws
        wr_raw = small2("wr_raw", [P, NK, NEXP])
        wr_h = small2("wr_h", [P, NK, NEXP], F32R)
        wr_l = small2("wr_l", [P, NK, NEXP], F32R)
        br_bc = small2("br_bc", [P, NEXP])
        slot_no = small2("slot_no", [P, P])
        onehot = [small2(f"onehot{n}", [P, NT, P]) for n in range(2)]
        scores = small2("scores", [P, NT, NEXP])
        chosen = small2("chosen", [P, NT, NEXP])
        pos = small2("pos", [P, NT, NU])
        table = small2("table", [P, NT, NU, 3])
        rtmp = small2("rtmp", [P, NT, NEXP])
        at_y = spot2[0]
        sel8 = small2("sel8", [P, NT, NGRP, 8])
        grp = small2("grp", [P, NT, NGRP])
        gtop = small2("gtop", [P, NT, 8])
        gidx = small2("gidx", [P, NT, 8], U32)
        gidf = small2("gidf", [P, NT, 8])
        geq = small2("geq", [P, NT, 8])
        gmask = small2("gmask", [P, NT, 8])
        iota8 = small2("iota8", [P, 8])
        etop = small2("etop", [P, NT, 8])
        wsum = small2("wsum", [P, NT])
        gtok = small2("gtok", [P, NT])
        stok = small2("stok", [P, NT])
        cmax = small2("cmax", [P, 1])
        spot2[0] = at_y
        y_sb = [small2(f"y_sb{n}", [P, D]) for n in range(2)]
        spot2[0] = max(spot2[0], at_y + 8 * KB)
        load_max = small2("load_max", [P, 1], I32)
        sg = small2("sg", [P, DE])
        hid = small2("hid", [P, DE])
        hidT = small2("hidT", [P, 2, P])
        ixg = [small2(f"ixg{n}", [P, 1], U32) for n in range(4)]
        ixs = [small2(f"ixs{n}", [P, 1], U32) for n in range(4)]
        cw = [small2(f"cw{n}", [P, 1]) for n in range(4)]
        stat2 = small2("stat2", [P, NT, 2, 6])
        mv2 = small2("mv2", [P, NT, 2])
        rstd2 = small2("rstd2", [P, NT])
        assert ARENA + spot2[0] <= nc.sbuf_usable_end, (ARENA + spot2[0], nc.sbuf_usable_end)
        yt = [sb(f"yt{n}", [P, TOPK, D], F32, at) for n, at in enumerate((at_r4, 0))]
        spot2[0] = at_ws
        sgp = small2("sgp", [P, NT, D])
        p_in = small2("p_in", [P, NT, 2 * P])
        hs = sb("hs", [P, NT, DE], F32, spot2[0] - 4 * NT * DE)
        pT_h = small2("pT_h", [P, 2, SEQ], F32R)
        hsT_h = sb("hsT_h", [P, 2, SEQ], F32R, spot2[0] - 4 * KB)
        pT_l = small2("pT_l", [P, 2, SEQ], F32R)
        hsT_l = sb("hsT_l", [P, 2, SEQ], F32R, spot2[0] - 4 * KB)
        sg_s = small2("sg_s", [P, NT, DE])
        stat3 = small2("stat3", [P, NT, 2, 6])
        mv3 = small2("mv3", [P, NT, 2])
        rstd3 = small2("rstd3", [P, NT])
        assert ARENA + spot2[0] <= nc.sbuf_usable_end
        BIG = 2 * SEQ * TOPK

        assert ARENA + spot[0] <= nc.sbuf_usable_end, (ARENA + spot[0], nc.sbuf_usable_end)

        ps = ctx.enter_context(nc.psum_tensor("ps", [P, 4, W], F32))
        aux = ctx.enter_context(nc.psum_tensor("aux", [P, 4, W], F32))

        def tiles(bank):
            return aux[:, bank, :].rearrange("p (t c) -> p t c", t=NT)

        def over_free(col, shape):
            return col.unsqueeze(len(shape) - 1).to_broadcast(shape)

        KINDS = ["qk", "vm", "v", "u", "ga", "pa", "o", "gb", "pb", "out"]
        FEATURE = {"qk", "u", "ga", "pa", "gb", "pb"}
        source = {"qk": (A["w_in"], C_Q), "vm": (A["w_in"], C_VM), "v": (A["w_in"], C_V),
                  "u": (A["w_in"], C_U), "ga": (A["w_in"], C_GA), "pa": (A["w_pa"], 0),
                  "o": (A["w_in"], C_O), "gb": (A["w_in"], C_GB), "pb": (A["w_pb"], 0),
                  "out": (A["w_out"], 0)}
        first_chunk = {k: 2 * n for n, k in enumerate(KINDS)}
        NCHUNK = 2 * len(KINDS)

        x_landed = [sem(f"x_landed{t}") for t in range(NT)]
        const_ready = sem("const_ready")
        gate_w_landed = sem("gate_w_landed")
        vec_landed = sem("vec_landed")
        ws_landed = sem("ws_landed")
        bs_landed = sem("bs_landed")
        bias_landed = [sem(f"bias_landed{n}") for n in range(5)]
        xres_landed = sem("xres_landed")
        raw_landed = [sem(f"raw_landed{s}") for s in range(2)]
        hi_ready = sem("hi_ready")
        lo_ready = sem("lo_ready")
        slice_done = sem("slice_done")
        drained = sem("drained")

        def drains(kind, chunk=1, t=3):
            return 4 * (first_chunk[kind] + chunk) + t + 1

        act_step = sem("act_step")
        dve_step = sem("dve_step")
        pool_step = sem("pool_step")
        xt_done = sem("xt_done")
        xh_ready = sem("xh_ready")
        xl_ready = sem("xl_ready")
        gw_hi = sem("gw_hi")
        gw_lo = sem("gw_lo")
        gates_done = sem("gates_done")
        gates_read = sem("gates_read")
        gate_abs = sem("gate_abs")
        gate_log = sem("gate_log")
        exp_asked = sem("exp_asked")
        exp_given = sem("exp_given")
        vec_done = sem("vec_done")
        bcol_ready = sem("bcol_ready")
        wst_done = sem("wst_done")
        wst_ready = sem("wst_ready")
        rows_ready = sem("rows_ready")
        cols_done = sem("cols_done")
        cols_ready = sem("cols_ready")
        a_done = sem("a_done")
        a_read = sem("a_read")
        arg_ready = sem("arg_ready")
        wexp_ready = sem("wexp_ready")
        wmask_ready = sem("wmask_ready")
        head_ready = sem("head_ready")
        kv_done = sem("kv_done")
        state_ready = sem("state_ready")
        num_done = sem("num_done")
        num_den = sem("num_den")
        num_read = sem("num_read")
        v_biased = sem("v_biased")
        v_ready = sem("v_ready")
        o_biased = sem("o_biased")
        var_ready = sem("var_ready")
        std_ready = sem("std_ready")
        vn_ready = sem("vn_ready")
        rsum_done = sem("rsum_done")
        rsum_read = sem("rsum_read")
        mixed_read = sem("mixed_read")
        mixed_done = sem("mixed_done")
        a_ready = sem("a_ready")
        ah_ready = sem("ah_ready")
        al_ready = sem("al_ready")
        ms_ready = sem("ms_ready")
        rms_ready = sem("rms_ready")
        mb_ready = sem("mb_ready")
        mt_done = sem("mt_done")
        mh_ready = sem("mh_ready")
        ml_ready = sem("ml_ready")
        yh_ready = sem("yh_ready")
        yl_ready = sem("yl_ready")
        y_ready = sem("y_ready")

        wr_landed = sem("wr_landed")
        wr_hi = sem("wr_hi")
        wr_lo = sem("wr_lo")
        var2_ready = sem("var2_ready")
        std2_ready = sem("std2_ready")
        x1_ready = sem("x1_ready")
        x1_stored = sem("x1_stored")
        x1t_done = sem("x1t_done")
        x1h_ready = sem("x1h_ready")
        x1l_ready = sem("x1l_ready")
        router_done = sem("router_done")
        scores_ready = sem("scores_ready")
        route_const = sem("route_const")
        chosen_ready = sem("chosen_ready")
        pos_done = sem("pos_done")
        slots_moved = sem("slots_moved")
        table_ready = sem("table_ready")
        load_ready = sem("load_ready")
        gu_landed = [sem(f"gu_landed{j}") for j in range(4)]
        dn_landed = [sem(f"dn_landed{j}") for j in range(4)]
        onehot_ready = sem("onehot_ready")
        list_done = sem("list_done")
        list_ready = sem("list_ready")
        gathered = [sem(f"gathered{n}") for n in range(2)]
        xgt_done = sem("xgt_done")
        xgt_act = sem("xgt_act")
        xgt_dve = sem("xgt_dve")
        gu_done = sem("gu_done")
        silu_ready = sem("silu_ready")
        hid_ready = sem("hid_ready")
        hidt_done = sem("hidt_done")
        hidt_ready = sem("hidt_ready")
        dn_done = sem("dn_done")
        y_act = sem("y_act")
        y_dve = sem("y_dve")
        scattered = [sem(f"scattered{n}") for n in range(2)]
        routed_done = sem("routed_done")
        experts_over = sem("experts_over")
        bpg_landed = sem("bpg_landed")
        p_landed = sem("p_landed")
        pt_done = sem("pt_done")
        ph_ready = sem("ph_ready")
        pl_ready = sem("pl_ready")
        pg_read = sem("pg_read")
        pg_ready = sem("pg_ready")
        wp_read = sem("wp_read")
        wp_added = sem("wp_added")
        sh_silu = sem("sh_silu")
        sh_ready = sem("sh_ready")
        ht_done = sem("ht_done")
        hh_ready = sem("hh_ready")
        hl_ready = sem("hl_ready")
        ds_added = sem("ds_added")
        ln2_landed = sem("ln2_landed")
        y_landed = [sem(f"y_landed{n}") for n in range(2)]
        y_summed = sem("y_summed")
        var3_ready = sem("var3_ready")
        std3_ready = sem("std3_ready")
        out_ready = sem("out_ready")
        out_stored = sem("out_stored")

        block = ctx.enter_context(nc.Block())

        def rows_of(w, half, col, n=W):
            return w[half * HK * P:(half + 1) * HK * P, bass.ds(col, n)].rearrange(
                "(k p) n -> p k n", p=P)

        @block.sync
        def _(sp):
            def wait_in_loop(s, value):
                value = sp.to_reg(value)
                sp.wait_ge(x_landed[0], 16)
                sp.wait_ge(s, value)

            for t in range(NT):
                sp.dma_start(x_in[:, t, :], A["x"][t * P:(t + 1) * P, :]).then_inc(x_landed[t], 16)
            for kind in KINDS:
                w, col = source[kind]
                c0 = first_chunk[kind]
                if kind == KINDS[0]:
                    for c in range(2):
                        for s in range(2):
                            if c:
                                sp.wait_ge(lo_ready, s + 1)
                            sp.dma_start(raw[s][:, :, :], rows_of(w, s, col + c * W)).then_inc(raw_landed[s], 16)
                    continue
                with sp.Fori(0, 2) as i:
                    for s in range(2):
                        wait_in_loop(lo_ready, 2 * c0 + s - 1 + i * 2)
                        sp.dma_start(raw[s][:, :, :], rows_of(w, s, col + i * W)).then_inc(raw_landed[s], 16)

            def gu_load(e, j):
                for n, w in enumerate(("w_gate_e", "w_up_e")):
                    sp.dma_start(gu[j][:, :, n * DE:(n + 1) * DE],
                                 A[w][bass.ds(e, 1)].rearrange("o (p k) f -> p (o k) f", k=NK)).then_inc(gu_landed[j], 16)

            def dn_load(e, j):
                sp.dma_start(dn[j][:, :, :], A["w_down_e"][bass.ds(e, 1)].rearrange("o (p k) f -> p (o k) f", k=2)
                             ).then_inc(dn_landed[j], 16)

            def weights_of_pass(ps_no, first=False):
                for j in range(4):
                    if first and j == 0:
                        sp.wait_ge(ml_ready, NK)
                        sp.wait_ge(y_ready, 8)
                        sp.wait_ge(yl_ready, 8)
                    if first and j == 1:
                        sp.wait_ge(slice_done, 8 * NCHUNK)
                    gu_load(j, j)
                    dn_load(j, j)
                with sp.Fori(0, NEXP // 4 - 1) as i:
                    for j in range(4):
                        wait_in_loop(gu_done, ps_no * NEXP + 4 * i + j + 1)
                        gu_load(4 * i + (4 + j), j)
                        wait_in_loop(dn_done, ps_no * NEXP + 4 * i + j + 1)
                        dn_load(4 * i + (4 + j), j)
                wait_in_loop(gu_done, (ps_no + 1) * NEXP)
                wait_in_loop(dn_done, (ps_no + 1) * NEXP)

            weights_of_pass(0, first=True)
            sp.wait_ge(load_ready, 1)
            with sp.If(sp.value_load(load_max[0:1, 0:1], min_val=0, max_val=SEQ) > P):
                with sp.Fori(1, NT) as ps_no:
                    weights_of_pass(ps_no)
            h = 2 * NCHUNK

            def tail_half(g, loads):
                if g >= h + 2:
                    sp.wait_ge(lo_ready, g - 1)
                for dst, src in loads:
                    sp.dma_start(dst, src).then_inc(raw_landed[g % 2], 16)

            for c in range(2):
                for s in range(2):
                    tail_half(h + 2 * c + s, [(raw[s][:, :, :], A["w_pg"][s * HK * P:(s + 1) * HK * P, c * W:(c + 1) * W
                                               ].rearrange("(k p) n -> p k n", p=P))])
            tail_half(h + 4, [(raw[0][:, :, :].rearrange("p (k a) n -> p k (a n)", k=2),
                               A["w_p"].rearrange("(k p) n -> p k n", p=P))])
            for s in range(2):
                g = h + 5 + s
                tail_half(g, [(raw[g % 2][:, :, n * DE:(n + 1) * DE],
                               A[w][s * HK * P:(s + 1) * HK * P, :].rearrange("(k p) n -> p k n", p=P))
                              for n, w in enumerate(("w_gate_s", "w_up_s"))])
            tail_half(h + 7, [(raw[1][:, :, :].rearrange("p (k a) n -> p k (a n)", k=2),
                               A["w_down_s"].rearrange("(k p) n -> p k n", p=P))])
            sp.wait_ge(routed_done, 1)
            sp.wait_ge(experts_over, 2)
            for t in range(NT):
                if t >= 2:
                    sp.wait_ge(y_summed, t - 1)
                sp.dma_start(yt[t % 2][:, :, :], y_rows[t * P * TOPK:(t + 1) * P * TOPK, :].rearrange(
                    "(p k) d -> p k d", k=TOPK)).then_inc(y_landed[t % 2], 16)
            for t in range(NT):
                sp.wait_ge(out_ready, t + 1)
                sp.dma_start(out[t * P:(t + 1) * P, :], xres[:, t, :]).then_inc(out_stored, 16)
            sp.wait_ge(out_stored, 16 * NT)

        @block.gpsimd
        def _(pool):
            step = Count(pool, pool_step)
            step.inc(nc.gpsimd.memset(ident[:, :], 0.0))
            step.inc(nc.gpsimd.memset(intra[:, :], 1.0))
            step.inc(nc.gpsimd.memset(sel[:, :, :], 0.0))
            step.inc(nc.gpsimd.memset(r_one[:, :], 1.0))
            step.inc(nc.gpsimd.memset(r_neg[:, :], 0.0))
            step.link(nc.gpsimd.memset(wg_raw[:, :, :], 0.0))
            for n, c in enumerate((C_I, C_F)):
                pool.dma_start(wg_raw[:, :, 32 * n:32 * n + MH],
                               A["w_in"][:, c:c + MH].rearrange("(k p) n -> p k n", p=P)).then_inc(gate_w_landed, 16)
            step.inc(nc.gpsimd.affine_select(out=ident[:, :], in_=ident[:, :], compare_op=ALU.not_equal, fill=1.0,
                                             base=0, pattern=[[-1, P]], channel_multiplier=1))
            step.inc(nc.gpsimd.affine_select(out=intra[:, :], in_=intra[:, :], compare_op=ALU.is_ge, fill=0.0,
                                             base=0, pattern=[[1, P]], channel_multiplier=-1))
            step.inc(nc.gpsimd.affine_select(out=sel[:, :, :], in_=sel[:, :, :], compare_op=ALU.not_equal, fill=1.0,
                                             base=0, pattern=[[-1, MH], [0, P]], channel_multiplier=1))
            step.inc(nc.gpsimd.memset(r_one[:, :].rearrange("p (c l) -> p c l", l=CHUNK)[:, :, 0:1], 0.0))
            step.link(nc.gpsimd.memset(r_neg[:, :].rearrange("p (c l) -> p c l", l=CHUNK)[:, :, 0:1], BIG_NEG))
            nc.gpsimd.memset(intra[0:CHUNK, CHUNK:P], 0.0).then_inc(const_ready, 1)
            nc.gpsimd.memset(ones[:, :], 1.0).then_inc(const_ready, 1)
            nc.gpsimd.memset(q_pad[:, :, :, :], 0.0).then_inc(const_ready, 1)
            nc.gpsimd.memset(m_row[:, 0:1], 0.0).then_inc(const_ready, 1)
            nc.gpsimd.memset(eps_ln[:, :], LN_EPS).then_inc(const_ready, 1)
            nc.gpsimd.memset(eps_rms[:, :], RMS_EPS).then_inc(const_ready, 1)
            nc.gpsimd.memset(vme[:, :, :, MV:MVE], 1.0).then_inc(const_ready, 1)
            pool.wait_ge(gates_done, 1)
            nc.gpsimd.memset(state[:, 0, :], 0.0).then_inc(const_ready, 1)
            for h in range(MH):
                pool.wait_ge(wexp_ready, h + 1)
                nc.gpsimd.tensor_tensor(wexp[:, :, :], wexp[:, :, :],
                                        intra[:, :].unsqueeze(1).to_broadcast([P, NT, P]),
                                        ALU.mult).then_inc(wmask_ready, 1)
            pool.wait_ge(wmask_ready, MH)
            pool.wait_ge(ml_ready, NK)
            pool.wait_ge(y_ready, 8)
            step.inc(nc.gpsimd.memset(before[:, :], 1.0))
            step.inc(nc.gpsimd.memset(pos[:, :, :], -1.0))
            step.link(nc.gpsimd.memset(table[:, :, :, :], 0.0))
            nc.gpsimd.affine_select(out=before[:, :], in_=before[:, :], compare_op=ALU.is_gt, fill=0.0, base=0,
                                    pattern=[[1, P]], channel_multiplier=-1).then_inc(route_const, 1)
            for dst, pattern, base, cm in ((slot_no, [[1, P]], 0, 0), (iota8, [[1, 8]], 0, 0),
                                           (gtok, [[P, NT]], -BIG, 1), (stok, [[P * TOPK, NT]], -BIG - 1, TOPK)):
                nc.gpsimd.iota(dst[:, :], pattern=pattern, base=base, channel_multiplier=cm,
                               allow_small_or_imprecise_dtypes=True).then_inc(route_const, 1)
            pool.wait_ge(slice_done, 8 * NCHUNK)
            step.inc(nc.gpsimd.memset(xg[0][:, :], 0.0))
            step.link(nc.gpsimd.memset(xg[1][:, :], 0.0))
            pool.wait_ge(x1_stored, 16 * NT)

            def wait_for(*waits):
                values = [pool.to_reg(value) for _, value in waits]
                pool.wait_ge(x1_stored, 16 * NT)
                for (s, _), value in zip(waits, values):
                    pool.wait_ge(s, value)

            last_token, last_row = pool.to_reg(SEQ - 1), pool.to_reg(SEQ * TOPK - 1)

            def gather(n, q):
                pool.indirect_dma_start(xg[n][:, :], None, x1_rows, bass.IndirectOffsetOnAxis(ixg[q][:, 0:1], 0),
                                        bounds_check=last_token, oob_is_err=False).then_inc(gathered[n], 16)

            def rows_of_pass(ps_no):
                for n in range(2):
                    wait_for((list_ready, ps_no * NU + n + 1))
                    gather(n, n)

                def scatter(v, j):
                    wait_for((y_act, ps_no * NEXP + v + 1), (y_dve, ps_no * NEXP + v + 1))
                    pool.indirect_dma_start(y_rows, bass.IndirectOffsetOnAxis(ixs[j][:, 0:1], 0), y_sb[j % 2][:, :],
                                            None, bounds_check=last_row, oob_is_err=False).then_inc(scattered[j % 2], 16)

                def expert(u, j, r):
                    wait_for((list_ready, ps_no * NU + u + 3), (xgt_done, ps_no * (NEXP + 1) + u + 1))
                    gather(j % 2, (j + 2) % 4)
                    if j or not isinstance(u, int):
                        scatter(u - 1, (j - 1) % 4)

                experts_in_order(pool, expert, NEXP)
                scatter(NEXP - 1, 3)
                wait_for(*((gathered[n], (ps_no + 1) * (16 * NU // 2)) for n in range(2)),
                         *((scattered[n], (ps_no + 1) * (16 * NEXP // 2)) for n in range(2)),
                         (xgt_done, (ps_no + 1) * (NEXP + 1)))

            rows_of_pass(0)
            pool.wait_ge(load_ready, 1)
            with pool.If(pool.value_load(load_max[0:1, 0:1], min_val=0, max_val=SEQ) > P):
                with pool.Fori(1, NT) as ps_no:
                    rows_of_pass(ps_no)
            nc.gpsimd.memset(mark[:, 0:1], 0.0).then_inc(routed_done, 1)

        @block.scalar
        def _(act):
            step = Count(act, act_step)

            def hi_split(s, landed, sliced=0):
                act.wait_ge(raw_landed[s], landed)
                wait_any(act, slice_done, sliced)
                nc.scalar.activation(w_h[s][:, :, :], raw[s][:, :, :], ACT.Copy).then_inc(hi_ready, 1)

            def split_ahead(c, last=False):
                hi_split(1, 16 * c + 16, 8 * c)
                if not last:
                    hi_split(0, 16 * c + 32, 8 * c + 4)

            act.dma_start(bif[:, 0:1], A["b_in"][C_I:C_I + MH].unsqueeze(1)).then_inc(vec_landed, 16)
            act.dma_start(bif[:, 1:2], A["b_in"][C_F:C_F + MH].unsqueeze(1)).then_inc(vec_landed, 16)
            for n, (v, c) in enumerate([("b_in", C_Q), ("b_in", C_U), ("b_in", C_GA), ("b_in", C_GB),
                                        ("sg_ln_g", 0), ("sg_ln_b", 0), ("mh_g", 0)]):
                act.dma_start(vec[n * NK:(n + 1) * NK, :],
                              A[v][c:c + D].rearrange("(r c) -> r c", c=P)).then_inc(vec_landed, 16)
            act.dma_start(ws_in[:, :, :], A["w_s"].rearrange("g t s -> t g s")).then_inc(ws_landed, 16)
            act.dma_start(add_bc[:, :, :], A["b_s"].partition_broadcast(P)).then_inc(bs_landed, 16)
            act.dma_start(bias_bc[0][:, :], A["b_in"][C_VM:C_VM + D].partition_broadcast(P)).then_inc(bias_landed[0], 16)
            act.dma_start(bias_bc[1][:, :], A["b_in"][C_V:C_V + D].partition_broadcast(P)).then_inc(bias_landed[1], 16)

            for k in range(NK):
                act.wait_ge(xt_done, k + 1)
                nc.scalar.activation(xT_h[:, k, :], aux[:, k % 4, :], ACT.Copy).then_inc(xh_ready, 1)
            act.wait_ge(gate_w_landed, 32)
            nc.scalar.activation(wg_h[:, :, :], wg_raw[:, :, :], ACT.Copy).then_inc(gw_hi, 1)
            act.wait_ge(bcol_ready, 1)
            hi_split(0, 16)

            def gate_rows():
                act.wait_ge(vec_landed, 16 * 9)
                act.wait_ge(gates_done, 1)
                nc.scalar.activation(r_a[:, :], aux[0:MH, 0, :], ACT.Identity, bias=bif[:, 0:1]).then_inc(gates_read, 1)
                nc.scalar.activation(r_f[:, :], aux[32:32 + MH, 0, :], ACT.Identity,
                                     bias=bif[:, 1:2]).then_inc(gates_read, 1)
                act.wait_ge(gate_abs, 1)
                step.link(nc.scalar.activation(r_t[:, :], r_t[:, :], ACT.Exp, scale=-1.0))
                nc.scalar.activation(r_t[:, :], r_t[:, :], ACT.Ln, bias=ones[0:MH, 0:1]).then_inc(gate_log, 1)
                for n, (r, scale) in enumerate([(win_row, 1.0), (r_f, 1.0), (r_em, -1.0), (dec_row, 1.0)]):
                    act.wait_ge(exp_asked, n + 1)
                    nc.scalar.activation(r[:, :], r[:, :], ACT.Exp, scale=scale).then_inc(rows_ready, 1)

            def decay_matrix(h):
                act.wait_ge(arg_ready, h + 1)
                nc.scalar.activation(wexp[:, :, :], wexp[:, :, :], ACT.Exp).then_inc(wexp_ready, 1)

            def numerators(h):
                for t in range(NT):
                    act.wait_ge(num_den, NT * h + t + 1)
                    nc.scalar.activation(vme[:, t, h, 0:MV], aux[:, t, 0:MV], ACT.Copy)
                    act.wait_ge(num_read, NT * h + t)
                    nc.scalar.activation(junk[:, :], aux[:, t, 0:MV], ACT.Square,
                                         accum_out=ssq[:, t, h:h + 1]).then_inc(num_read, 1)

            for kind in KINDS:
                c0 = first_chunk[kind]
                if kind == "ga":
                    act.wait_ge(mixed_done, GG)
                    for g in range(GG):
                        act.wait_ge(a_ready, g + 1)
                        nc.scalar.activation(aT_h[:, g, :], uT[:, g, :], ACT.Copy).then_inc(ah_ready, 1)
                if kind == "o":
                    act.wait_ge(drained, drains("vm"))
                    act.dma_start(bias_bc[0][:, :], A["b_in"][C_O:C_O + D].partition_broadcast(P)).then_inc(
                        bias_landed[2], 16)
                    act.wait_ge(drained, drains("v"))
                    act.dma_start(bias_bc[1][:, :], A["ln1_g"].partition_broadcast(P)).then_inc(bias_landed[3], 16)

                if kind == "out":
                    act.wait_ge(y_ready, 8)
                    act.wait_ge(ml_ready, NK)
                    act.dma_start(wr_raw[:, :, :], A["w_router"].rearrange("(k p) e -> p k e", p=P)).then_inc(wr_landed, 16)
                    act.dma_start(br_bc[:, :], A["b_router"].partition_broadcast(P)).then_inc(wr_landed, 16)

                def chunk(i, last=False):
                    c = c0 + i
                    split_ahead(c, last)
                    if kind == "ga":
                        act.wait_ge(al_ready, GG)
                    for t in range(4):
                        if kind in ("qk", "u", "ga", "gb"):
                            act.wait_ge(slice_done, 8 * c + 5 + t)
                            dst, func, b = {"qk": (qkT, ACT.Identity, B_QK), "u": (uT, ACT.Gelu, B_U),
                                            "ga": (yT, ACT.Sigmoid, B_GA), "gb": (gbT, ACT.Sigmoid, B_GB)}[kind]
                            if kind == "qk":
                                to = qkT[:, bass.ds(i, 1), t, :].rearrange("p a n -> p (a n)")
                            else:
                                to = dst[:, bass.ds(4 * i + t, 1), :].rearrange("p a n -> p (a n)")
                            nc.scalar.activation(to, ps[:, t, :], func,
                                                 bias=bcol[:, bass.ds(b + 4 * i + t, 1)]).then_inc(drained, 1)
                        elif kind == "v":
                            act.wait_ge(drained, drains("v", i, t))
                            part = v_sb[:, t, bass.ds(i * W, W)]
                            nc.scalar.activation(part, part, ACT.Gelu).then_inc(v_ready, 1)
                        elif kind == "o":
                            act.wait_ge(drained, drains("o", i, t))
                            part = osig[:, t, bass.ds(i * W, W)]
                            nc.scalar.activation(part, part, ACT.Sigmoid).then_inc(o_biased, 1)
                        elif kind == "pb":
                            act.wait_ge(y_ready, 4 * i + t + 1)
                            part = yT[:, bass.ds(4 * i + t, 1), :]
                            nc.scalar.activation(yT_h[:, bass.ds(4 * i + t, 1), :], part, ACT.Copy).then_inc(yh_ready, 1)

                if kind == KINDS[0]:
                    chunk(0)
                    chunk(1)
                elif kind != "out":
                    with act.Fori(0, 2) as i:
                        chunk(i)
                else:
                    chunk(0)
                    chunk(1, last=True)

                if kind == "qk":
                    gate_rows()
                if kind == "vm":
                    decay_matrix(0)
                if kind == "v":
                    numerators(0)
                    decay_matrix(1)
                    act.wait_ge(var_ready, NT)
                    nc.scalar.activation(rstd[:, :], mv[:, :, 1:2].rearrange("p t o -> p (t o)"), ACT.Sqrt,
                                         bias=eps_ln[:, :]).then_inc(std_ready, 1)
                if kind == "u":
                    numerators(1)
                    decay_matrix(2)
                if kind == "ga":
                    numerators(2)
                    decay_matrix(3)
                if kind == "pa":
                    numerators(3)
                if kind == "o":
                    act.wait_ge(drained, drains("o"))
                    act.dma_start(bias_bc[0][:, :], A["ln1_b"].partition_broadcast(P)).then_inc(bias_landed[4], 16)
                    act.wait_ge(ms_ready, 1)
                    nc.scalar.activation(hs2[:, :, :], hs2[:, :, :], ACT.Sqrt, bias=eps_rms[:, :]).then_inc(rms_ready, 1)
                    for k in range(NK):
                        act.wait_ge(mt_done, k + 1)
                        nc.scalar.activation(mT_h[:, k, :], aux[:, k % 4, :], ACT.Copy,
                                             scale=bcol[:, B_MG + k:B_MG + k + 1]).then_inc(mh_ready, 1)
                    for t in range(NT):
                        act.dma_start(xres[:, t, :], A["x"][t * P:(t + 1) * P, :]).then_inc(xres_landed, 16)

            act.wait_ge(drained, drains("out"))

            def std2(t):
                act.wait_ge(var2_ready, t + 1)
                nc.scalar.activation(rstd2[:, t:t + 1], mv2[:, t, 1:2], ACT.Sqrt, bias=eps_ln[:, :]).then_inc(std2_ready, 1)

            std2(0)
            act.wait_ge(wr_landed, 32)
            nc.scalar.activation(wr_h[:, :, :], wr_raw[:, :, :], ACT.Copy).then_inc(wr_hi, 1)
            for t in range(NT):
                act.wait_ge(x1_ready, t + 1)
                act.dma_start(x1_rows[t * P:(t + 1) * P, :], xres[:, t, :]).then_inc(x1_stored, 16)
                if t + 1 < NT:
                    std2(t + 1)
                for n in range(2):
                    act.wait_ge(x1t_done, 2 * t + n + 1)
                    nc.scalar.activation(x1T_h[:, n * HK:(n + 1) * HK, t * P:(t + 1) * P], tiles((2 * t + n) % 4),
                                         ACT.Copy).then_inc(x1h_ready, 1)
            act.wait_ge(router_done, NT)
            nc.scalar.activation(scores[:, :, :], ps[:, 0, 0:NT * NEXP].rearrange("p (t e) -> p t e", t=NT),
                                 ACT.Sigmoid).then_inc(scores_ready, 1)

            def xgt_copy(n, count):
                act.wait_ge(xgt_done, count)
                nc.scalar.activation(xgT[n][:, 0:HK, :], ps[:, 0, :].rearrange("p (k s) -> p k s", k=HK),
                                     ACT.Copy).then_inc(xgt_act, 1)

            def experts_of_pass(ps_no):
                T0, E0, S0 = ps_no * (NEXP + 1), ps_no * NEXP, ps_no * (16 * NEXP // 2)

                def rows_out(v, n, scattered_before):
                    act.wait_ge(dn_done, E0 + v + 1)
                    wait_any(act, scattered[n], S0 + scattered_before)
                    nc.scalar.activation(y_sb[n][:, 0:W], aux[:, 2, :], ACT.Copy).then_inc(y_act, 1)

                def expert(u, j, r):
                    act.wait_ge(gu_done, E0 + u + 1)
                    nc.scalar.activation(sg[:, :], ps[:, 2, 0:DE], ACT.Silu).then_inc(silu_ready, 1)
                    xgt_copy((j + 1) % 2, T0 + u + 2)
                    if j or not isinstance(u, int):
                        rows_out(u - 1, (j - 1) % 2, 32 * r + 16 * ((j - 1) // 2))
                    act.wait_ge(hidt_done, E0 + u + 1)
                    nc.scalar.activation(hidT[:, :, :], aux[:, 0, 0:2 * P].rearrange("p (k s) -> p k s", k=2),
                                         ACT.Copy).then_inc(hidt_ready, 1)

                xgt_copy(0, T0 + 1)
                experts_in_order(act, expert, NEXP)
                rows_out(NEXP - 1, 1, 16 * (NEXP // 2 - 1))

            experts_of_pass(0)
            act.wait_ge(load_ready, 1)
            with act.If(act.value_load(load_max[0:1, 0:1], min_val=0, max_val=SEQ) > P):
                with act.Fori(1, NT) as ps_no:
                    experts_of_pass(ps_no)
            nc.scalar.activation(mark[:, 1:2], ones[:, 0:1], ACT.Copy).then_inc(experts_over, 1)

            act.wait_ge(experts_over, 2)
            act.wait_ge(routed_done, 1)
            act.dma_start(bias_bc[0][:, :], A["b_pg"].partition_broadcast(P)).then_inc(bpg_landed, 16)
            act.dma_start(p_in[:, :, :], A["p"].rearrange("(t p) n -> p t n", p=P)).then_inc(p_landed, 16)
            G = 2 * NCHUNK
            S = 8 * NCHUNK

            def hi_tail(n, landed):
                s = n % 2
                act.wait_ge(raw_landed[s], landed)
                if n >= 2:
                    act.wait_ge(slice_done, S + 4 * (n - 1))
                nc.scalar.activation(w_h[s][:, :, :], raw[s][:, :, :], ACT.Copy).then_inc(hi_ready, 1)

            R = 16 * NCHUNK
            hi_tail(0, R + 16)
            for k in range(2):
                act.wait_ge(pt_done, k + 1)
                nc.scalar.activation(pT_h[:, k, :], aux[:, k, :], ACT.Copy).then_inc(ph_ready, 1)
            hi_tail(1, R + 16)
            hi_tail(2, R + 32)
            for c in range(2):
                for t in range(NT):
                    act.wait_ge(pg_read, 4 * c + t + 1)
                    part = sgp[:, t, c * W:(c + 1) * W]
                    nc.scalar.activation(part, part, ACT.Sigmoid).then_inc(pg_ready, 1)
                if c == 0:
                    hi_tail(3, R + 32)
                    hi_tail(4, R + 48)
            hi_tail(5, R + 64)
            hi_tail(6, R + 80)
            act.dma_start(bias_bc[1][:, :], A["ln2_g"].partition_broadcast(P)).then_inc(ln2_landed, 16)
            act.wait_ge(pg_read, 8)
            act.dma_start(bias_bc[0][:, :], A["ln2_b"].partition_broadcast(P)).then_inc(ln2_landed, 16)
            hi_tail(7, R + 80)
            for t in range(NT):
                act.wait_ge(slice_done, S + 24 + t + 1)
                nc.scalar.activation(sg_s[:, t, :], ps[:, t, 0:DE], ACT.Silu).then_inc(sh_silu, 1)
            for k in range(2):
                act.wait_ge(ht_done, k + 1)
                nc.scalar.activation(hsT_h[:, k, :], aux[:, k, :], ACT.Copy).then_inc(hh_ready, 1)
            for t in range(NT):
                act.wait_ge(var3_ready, t + 1)
                nc.scalar.activation(rstd3[:, t:t + 1], mv3[:, t, 1:2], ACT.Sqrt, bias=eps_ln[:, :]).then_inc(std3_ready, 1)

        @block.vector
        def _(dve):
            step = Count(dve, dve_step)
            TT = nc.vector.tensor_tensor
            STT = nc.vector.scalar_tensor_tensor

            def lo_split(s, rounded):
                dve.wait_ge(hi_ready, rounded)
                TT(w_l[s][:, :, :], raw[s][:, :, :], w_h[s][:, :, :].bitcast(F32), ALU.subtract).then_inc(lo_ready, 1)

            for k in range(NK):
                dve.wait_ge(xh_ready, k + 1)
                TT(xT_l[:, k, :], aux[:, k % 4, :], xT_h[:, k, :].bitcast(F32), ALU.subtract).then_inc(xl_ready, 1)
            dve.wait_ge(gw_hi, 1)
            TT(wg_l[:, :, :], wg_raw[:, :, :], wg_h[:, :, :].bitcast(F32), ALU.subtract).then_inc(gw_lo, 1)
            dve.wait_ge(vec_done, 1)
            nc.vector.tensor_copy(bcol[:, :], aux[:, 1, 0:NROW]).then_inc(bcol_ready, 1)
            for n in range(2):
                dve.wait_ge(wst_done, n + 1)
                step.link(nc.vector.tensor_copy(wsT[:, 4 * n:4 * n + 4, :], tiles(2 + n)))
            nc.vector.memset(wsT[CHUNK:P, :, 0:CHUNK], 0.0).then_inc(wst_ready, 1)
            lo_split(0, 1)

            def gate_rows():
                blk = lambda r: r[:, :].rearrange("p (c l) -> p c l", l=CHUNK)
                last = lambda r: blk(r)[:, :, CHUNK - 1:CHUNK]
                prev = m_row[:, 0:NC].unsqueeze(2)
                dve.wait_ge(gates_read, 2)
                dve.wait_ge(const_ready, 7)
                STT(r_t[:, :], r_f[:, :], -1.0, r_f[:, :], ALU.mult, ALU.max).then_inc(gate_abs, 1)
                dve.wait_ge(gate_log, 1)
                step.link(STT(r_f[:, :], r_f[:, :], 0.0, r_t[:, :], ALU.min, ALU.subtract))
                step.link(nc.vector.tensor_tensor_scan(r_b[:, :], r_one[:, :], r_f[:, :], 0.0, ALU.mult, ALU.add))
                step.link(TT(r_a[:, :], r_a[:, :], r_b[:, :], ALU.subtract))
                step.link(nc.vector.tensor_tensor_scan(r_cm[:, :], r_neg[:, :], r_a[:, :], BIG_NEG, ALU.add, ALU.max))
                g3 = g_row[:, :].unsqueeze(2)
                step.link(TT(g3, last(r_b), last(r_cm), ALU.add))
                step.link(nc.vector.tensor_copy(dec_row[:, :].unsqueeze(2), last(r_b)))
                step.link(nc.vector.tensor_tensor_scan(m_row[:, 1:NC + 1], dec_row[:, :], g_row[:, :], 0.0,
                                                       ALU.add, ALU.max))
                step.link(TT(blk(u_row), blk(r_cm), prev.to_broadcast([MH, NC, CHUNK]), ALU.max))
                TT(blk(win_row), prev.to_broadcast([MH, NC, CHUNK]), blk(u_row), ALU.subtract).then_inc(exp_asked, 1)
                TT(blk(r_f), blk(r_a), last(u_row).to_broadcast([MH, NC, CHUNK]), ALU.subtract).then_inc(exp_asked, 1)
                TT(r_em[:, :], r_b[:, :], u_row[:, :], ALU.add).then_inc(exp_asked, 1)
                TT(dec_row[:, :].unsqueeze(2), prev, last(u_row), ALU.subtract).then_inc(exp_asked, 1)

            def token_columns():
                dve.wait_ge(cols_done, 2)
                nc.vector.tensor_copy(dec_bc[:, :, :], aux[:, 0, 0:MH * NC].rearrange("p (h c) -> p h c", h=MH)
                                      ).then_inc(cols_ready, 1)
                nc.vector.tensor_copy(cols[:, :, :], aux[:, 1, 0:NT * 3 * MH].rearrange(
                    "p (t c) -> p t c", t=NT)).then_inc(cols_ready, 1)
                dve.wait_ge(cols_ready, 2)
                dve.wait_ge(bs_landed, 16)
                dve.wait_ge(bcol_ready, 1)
                for g in range(GG):
                    dve.wait_ge(rsum_done, g // 4 + 1)
                    STT(add_bc[:, g, :], aux[:, 2 + g // 4, (g % 4) * P:(g % 4 + 1) * P],
                        bcol[:, B_SB + g:B_SB + g + 1], add_bc[:, g, :], ALU.mult, ALU.add).then_inc(rsum_read, 1)
                dve.wait_ge(rsum_read, GG)

            def head_inputs(h):
                full = [P, NT, P]
                a_col = over_free(cols[:, :, h:h + 1].rearrange("p t o -> p (t o)"), full)
                k_col = over_free(cols[:, :, MH + h:MH + h + 1].rearrange("p t o -> p (t o)"), full)
                dve.wait_ge(a_done, 4 * h + 4)
                if h:
                    dve.wait_ge(num_done, NT * h)
                step.link(TT(wexp[:, :, :], tiles(1), a_col, ALU.max))
                TT(wexp[:, :, :], a_col, wexp[:, :, :], ALU.subtract).then_inc(arg_ready, 1)
                TT(kw[:, :, :], tiles(3), k_col, ALU.mult).then_inc(head_ready, 1)
                dve.wait_ge(drained, drains("qk"))
                qT = qkT[:, 0, h, :].rearrange("p (t c l) -> p t c l", t=NT, l=CHUNK)
                win = aux[:, 2, :].rearrange("p (t c l) -> p t c l", t=NT, l=CHUNK)
                for c in range(2):
                    STT(q_pad[:, :, c, c * CHUNK:(c + 1) * CHUNK], qT[:, :, c, :], QK ** -0.5, win[:, :, c, :],
                        ALU.mult, ALU.mult).then_inc(head_ready, 1)
                dve.wait_ge(wmask_ready, h + 1)
                STT(wS[:, :, :], tiles(0), QK ** -0.5, wexp[:, :, :], ALU.mult, ALU.mult).then_inc(head_ready, 1)

            def head_states(h):
                dve.wait_ge(const_ready, 8)
                for c in range(NC - 1):
                    dve.wait_ge(kv_done, (NC - 1) * h + c + 1)
                    STT(state[:, c + 1, :], state[:, c, :], dec_bc[:, h, c:c + 1], aux[:, c % 4, 0:MVE],
                        ALU.mult, ALU.add).then_inc(state_ready, 1)
                    dve.wait_ge(state_ready, (NC - 1) * h + c + 1)

            def head_den(h):
                for t in range(NT):
                    dve.wait_ge(num_done, NT * h + t + 1)
                    d = den[:, t, h:h + 1]
                    step.link(TT(d, aux[:, t, MV:MVE], cols[:, t, 2 * MH + h:2 * MH + h + 1], ALU.max))
                    STT(d, aux[:, t, MV:MVE], -1.0, d, ALU.mult, ALU.max).then_inc(num_den, 1)

            for kind in KINDS:
                c0 = first_chunk[kind]
                if kind in ("vm", "v", "o"):
                    dve.wait_ge(bias_landed[{"vm": 0, "v": 1, "o": 2}[kind]], 16)
                if kind == "vm":
                    dve.wait_ge(const_ready, 7)
                if kind == "out":
                    dve.wait_ge(xres_landed, 16 * NT)
                if kind == "o":
                    dve.wait_ge(a_done, 16)

                def chunk(i, last=False):
                    c = c0 + i
                    lo_split(1, 2 * c + 2)
                    if not last:
                        lo_split(0, 2 * c + 3)
                    for t in range(4):
                        if kind in ("vm", "v", "o", "pa", "pb", "out"):
                            dve.wait_ge(slice_done, 8 * c + 5 + t)
                        feat = bass.ds(4 * i + t, 1)
                        bank = ps[:, t, :]
                        if kind == "vm":
                            TT(vme[:, t, bass.ds(2 * i, 2), 0:MV], bank.rearrange("p (h v) -> p h v", v=MV),
                               bias_bc[0][:, bass.ds(i * W, W)].rearrange("p (h v) -> p h v", v=MV),
                               ALU.add).then_inc(drained, 1)
                        elif kind in ("v", "o"):
                            dst, b = {"v": (v_sb, 1), "o": (osig, 0)}[kind]
                            TT(dst[:, t, bass.ds(i * W, W)], bank, bias_bc[b][:, bass.ds(i * W, W)],
                               ALU.add).then_inc(drained, 1)
                        elif kind == "pa":
                            dve.wait_ge(drained, drains("ga"))
                            part = yT[:, feat, :].rearrange("p a n -> p (a n)")
                            TT(part, bank, part, ALU.mult).then_inc(drained, 1)
                        elif kind == "pb":
                            dve.wait_ge(drained, drains("gb"))
                            part = yT[:, feat, :].rearrange("p a n -> p (a n)")
                            TT(tmp[:, :], bank, gbT[:, feat, :].rearrange("p a n -> p (a n)"),
                               ALU.mult).then_inc(drained, 1)
                            dve.wait_ge(drained, drains(kind, i, t))
                            TT(part, part, tmp[:, :], ALU.add).then_inc(y_ready, 1)
                            dve.wait_ge(y_ready, 4 * i + t + 1)
                        elif kind == "out":
                            part = xres[:, t, bass.ds(i * W, W)]
                            STT(part, part, ALPHA, bank, ALU.mult, ALU.add).then_inc(drained, 1)
                    if kind == "pb":
                        for t in range(4):
                            dve.wait_ge(yh_ready, 4 * i + t + 1)
                            feat = bass.ds(4 * i + t, 1)
                            TT(yT_l[:, feat, :], yT[:, feat, :], yT_h[:, feat, :].bitcast(F32),
                               ALU.subtract).then_inc(yl_ready, 1)

                if kind != "out":
                    with dve.Fori(0, 2) as i:
                        chunk(i)
                else:
                    chunk(0)
                    chunk(1, last=True)

                if kind == "qk":
                    gate_rows()
                if kind == "vm":
                    token_columns()
                    head_inputs(0)
                if kind == "v":
                    head_states(0)
                    head_den(0)
                    head_inputs(1)
                    dve.wait_ge(v_ready, 8)
                    for t in range(NT):
                        for n in range(2):
                            step.inc(nc.vector.bn_stats(stat[:, t, n, :], v_sb[:, t, n * W:(n + 1) * W]))
                    dve.wait_ge(dve_step, step.base + step.more)
                    for t in range(NT):
                        nc.vector.bn_aggr(mv[:, t, :], stat[:, t, :, :]).then_inc(var_ready, 1)
                    dve.wait_ge(var_ready, NT)
                    dve.wait_ge(std_ready, 1)
                    step.link(nc.vector.reciprocal(rstd[:, :], rstd[:, :]))
                    for t in range(NT):
                        nc.vector.tensor_scalar(v_sb[:, t, :], v_sb[:, t, :], mv[:, t, 0:1], rstd[:, t:t + 1],
                                                ALU.subtract, ALU.mult).then_inc(vn_ready, 1)
                if kind == "u":
                    dve.wait_ge(drained, drains("u"))
                    for g in range(GG):
                        dve.wait_ge(mixed_done, g + 1)
                        dve.wait_ge(a_ready, g)
                        STT(tmp[:, :].rearrange("p (t c) -> p t c", t=NT), tiles(g % 4),
                            bcol[:, B_SG + g:B_SG + g + 1], add_bc[:, g, :].unsqueeze(1).to_broadcast([P, NT, P]),
                            ALU.mult, ALU.add).then_inc(mixed_read, 1)
                        dve.wait_ge(mixed_read, g + 1)
                        TT(uT[:, g, :], uT[:, g, :], tmp[:, :], ALU.mult).then_inc(a_ready, 1)
                    head_states(1)
                    head_den(1)
                    head_inputs(2)
                    for g in range(GG):
                        dve.wait_ge(ah_ready, g + 1)
                        TT(aT_l[:, g, :], uT[:, g, :], aT_h[:, g, :].bitcast(F32), ALU.subtract).then_inc(al_ready, 1)
                if kind == "ga":
                    head_states(2)
                    head_den(2)
                    head_inputs(3)
                if kind == "pa":
                    head_states(3)
                    head_den(3)
                if kind == "o":
                    dve.wait_ge(num_read, NT * MH)
                    dve.wait_ge(num_den, NT * MH)
                    step.link(nc.vector.reciprocal(den[:, :, :], den[:, :, :]))
                    step.link(TT(hs2[:, :, :], den[:, :, :], den[:, :, :], ALU.mult))
                    STT(hs2[:, :, :], hs2[:, :, :], 1.0 / MV, ssq[:, :, :], ALU.mult, ALU.mult).then_inc(ms_ready, 1)
                    dve.wait_ge(rms_ready, 1)
                    step.link(nc.vector.reciprocal(hs2[:, :, :], hs2[:, :, :]))
                    step.link(TT(hsc[:, :, :], hs2[:, :, :], den[:, :, :], ALU.mult))
                    dve.wait_ge(o_biased, 8)
                    for t in range(NT):
                        for h in range(MH):
                            part = osig[:, t, h * MV:(h + 1) * MV]
                            STT(part, vme[:, t, h, 0:MV], hsc[:, t, h:h + 1], part, ALU.mult,
                                ALU.mult).then_inc(mb_ready, 1)
                    for k in range(NK):
                        dve.wait_ge(mh_ready, k + 1)
                        STT(mT_l[:, k, :], aux[:, k % 4, :], bcol[:, B_MG + k:B_MG + k + 1],
                            mT_h[:, k, :].bitcast(F32), ALU.mult, ALU.subtract).then_inc(ml_ready, 1)

            def norm(t, stat_, mv_, rstd_, var_sem, std_sem, count, last_sem):
                for n in range(2):
                    step.inc(nc.vector.bn_stats(stat_[:, t, n, :], xres[:, t, n * W:(n + 1) * W]))
                dve.wait_ge(dve_step, step.base + step.more)
                nc.vector.bn_aggr(mv_[:, t, :], stat_[:, t, :, :]).then_inc(var_sem, 1)
                dve.wait_ge(std_sem, count)
                r = rstd_[:, t:t + 1]
                step.link(nc.vector.reciprocal(r, r))
                step.link(nc.vector.tensor_scalar(xres[:, t, :], xres[:, t, :], mv_[:, t, 0:1], r, ALU.subtract, ALU.mult))
                step.link(TT(xres[:, t, :], xres[:, t, :], bias_bc[1][:, :], ALU.mult))
                TT(xres[:, t, :], xres[:, t, :], bias_bc[0][:, :], ALU.add).then_inc(last_sem, 1)

            dve.wait_ge(bias_landed[3], 16)
            dve.wait_ge(bias_landed[4], 16)
            dve.wait_ge(route_const, 5)
            dve.wait_ge(drained, drains("out"))

            def x1_low(t):
                for n in range(2):
                    dve.wait_ge(x1h_ready, 2 * t + n + 1)
                    part = (slice(None), slice(n * HK, (n + 1) * HK), slice(t * P, (t + 1) * P))
                    TT(x1T_l[part], tiles((2 * t + n) % 4), x1T_h[part].bitcast(F32), ALU.subtract).then_inc(x1l_ready, 1)

            for t in range(NT):
                norm(t, stat2, mv2, rstd2, var2_ready, std2_ready, t + 1, x1_ready)
                if t == 0:
                    dve.wait_ge(wr_hi, 1)
                    TT(wr_l[:, :, :], wr_raw[:, :, :], wr_h[:, :, :].bitcast(F32), ALU.subtract).then_inc(wr_lo, 1)
                else:
                    x1_low(t - 1)
            x1_low(NT - 1)

            full = [P, NT, NEXP]
            dve.wait_ge(scores_ready, 1)
            sel = sel8[:, :, :, :].rearrange("p t g e -> p t (g e)")
            best = rtmp[:, :, :].rearrange("p t (g e) -> p t g e", g=NGRP)
            step.link(TT(sel, scores[:, :, :], br_bc[:, :].unsqueeze(1).to_broadcast(full), ALU.add))
            for t in range(NT):
                for g in range(NGRP):
                    step.inc(nc.vector.max(best[:, t, g, :], sel8[:, t, g, :]))
            dve.wait_ge(dve_step, step.base + step.more)
            step.link(TT(grp[:, :, :].unsqueeze(3), best[:, :, :, 0:1], best[:, :, :, 1:2], ALU.add))
            for t in range(NT):
                step.inc(nc.vector.max(gtop[:, t, :], grp[:, t, :]))
            dve.wait_ge(dve_step, step.base + step.more)
            for t in range(NT):
                step.inc(nc.vector.max_index(gidx[:, t, :], gtop[:, t, :], grp[:, t, :]))
            dve.wait_ge(dve_step, step.base + step.more)
            step.link(nc.vector.tensor_copy(gidf[:, :, :], gidx[:, :, :]))
            for n in range(TOPG):
                dst = gmask if n == 0 else geq
                step.link(TT(dst[:, :, :], iota8[:, :].unsqueeze(1).to_broadcast([P, NT, 8]),
                             gidf[:, :, n:n + 1].to_broadcast([P, NT, 8]), ALU.is_equal))
                if n:
                    step.link(TT(gmask[:, :, :], gmask[:, :, :], geq[:, :, :], ALU.add))
            step.link(TT(sel8[:, :, :, :], sel8[:, :, :, :], gmask[:, :, :].unsqueeze(3).to_broadcast([P, NT, NGRP, 8]),
                         ALU.mult))
            step.link(nc.vector.tensor_scalar(gmask[:, :, :], gmask[:, :, :], -BIG_NEG, BIG_NEG, ALU.mult, ALU.add))
            step.link(TT(sel8[:, :, :, :], sel8[:, :, :, :], gmask[:, :, :].unsqueeze(3).to_broadcast([P, NT, NGRP, 8]),
                         ALU.add))
            for t in range(NT):
                step.inc(nc.vector.max(etop[:, t, :], sel[:, t, :]))
            dve.wait_ge(dve_step, step.base + step.more)
            for t in range(NT):
                step.inc(nc.vector.match_replace(rtmp[:, t, :], etop[:, t, :], sel[:, t, :], 3 * BIG_NEG))
            dve.wait_ge(dve_step, step.base + step.more)
            TT(chosen[:, :, :], rtmp[:, :, :], sel, ALU.not_equal).then_inc(chosen_ready, 1)
            dve.wait_ge(chosen_ready, 1)
            step.link(TT(scores[:, :, :], scores[:, :, :], chosen[:, :, :], ALU.mult))
            step.link(nc.vector.tensor_reduce(wsum[:, :], scores[:, :, :], AX.X, ALU.add))
            step.link(nc.vector.reciprocal(wsum[:, :], wsum[:, :]))
            step.inc(STT(table[:, :, 0:NEXP, 2], scores[:, :, :], ROUTE_SCALE, wsum[:, :].unsqueeze(2).to_broadcast(full),
                         ALU.mult, ALU.mult))
            for t in range(NT):
                step.inc(nc.vector.tensor_tensor_scan(rtmp[:, t, :], ones[:, 0:NEXP], chosen[:, t, :], 0.0, ALU.mult, ALU.add))
            dve.wait_ge(dve_step, step.base + step.more)
            for t in range(NT):
                step.inc(nc.vector.tensor_scalar(table[:, t, 0:NEXP, 0], rtmp[:, t, :], 0.0, gtok[:, t:t + 1], ALU.mult, ALU.add))
                step.inc(nc.vector.tensor_scalar(table[:, t, 0:NEXP, 1], rtmp[:, t, :], stok[:, t:t + 1], None, ALU.add))
            dve.wait_ge(pos_done, NT)
            step.link(STT(pos[:, :, 0:NEXP], ps[:, 1, 0:NT * NEXP].rearrange("p (t e) -> p t e", t=NT), 1.0,
                          chosen[:, :, :], ALU.add, ALU.mult))
            nc.vector.tensor_scalar(pos[:, :, 0:NEXP], pos[:, :, 0:NEXP], -1.0, None, ALU.add).then_inc(table_ready, 1)
            dve.wait_ge(table_ready, 1)
            dve.wait_ge(pos_done, NT + 1)
            step.link(nc.vector.tensor_reduce(cmax[:, :], ps[:, 2, 0:NEXP], AX.X, ALU.max))
            nc.vector.tensor_copy(load_max[:, :], cmax[:, :]).then_inc(load_ready, 1)
            dve.wait_ge(load_ready, 1)

            def onehot_of(n, e, count):
                wait_any(dve, list_done, count)
                TT(onehot[n][:, :, :], slot_no[:, :].unsqueeze(1).to_broadcast([P, NT, P]),
                   pos[:, :, bass.ds(e, 1)].to_broadcast([P, NT, P]), ALU.is_equal).then_inc(onehot_ready, 1)

            def list_of(q, count):
                dve.wait_ge(list_done, count)
                at = 4 * (q % 2)
                nc.vector.tensor_scalar(ixg[q][:, :], ps[:, 3, at:at + 1], float(BIG), None, ALU.add)
                nc.vector.tensor_scalar(ixs[q][:, :], ps[:, 3, at + 1:at + 2], float(BIG), None, ALU.add)
                nc.vector.tensor_copy(cw[q][:, :], ps[:, 3, at + 2:at + 3]).then_inc(list_ready, 1)

            def xgt_copy(n, count):
                dve.wait_ge(xgt_done, count)
                nc.vector.tensor_copy(xgT[n][:, HK:NK, :], ps[:, 1, :].rearrange("p (k s) -> p k s", k=HK)).then_inc(xgt_dve, 1)

            def experts_of_pass(ps_no, again=False):
                T0, E0, L0 = ps_no * (NEXP + 1), ps_no * NEXP, ps_no * NU
                for n in range(2):
                    onehot_of(n, n, L0)
                for n in range(2):
                    if again:
                        dve.wait_ge(gathered[n], ps_no * (16 * NU // 2))
                        dve.wait_ge(scattered[0], ps_no * (16 * NEXP // 2))
                        dve.wait_ge(scattered[1], ps_no * (16 * NEXP // 2))
                    list_of(n, L0 + n + 1)
                xgt_copy(0, T0 + 1)
                S0 = ps_no * (16 * NEXP // 2)

                def rows_out(v, n, scattered_before):
                    dve.wait_ge(dn_done, E0 + v + 1)
                    wait_any(dve, scattered[n], S0 + scattered_before)
                    nc.vector.tensor_copy(y_sb[n][:, W:2 * W], aux[:, 3, :]).then_inc(y_dve, 1)

                def expert(u, j, r):
                    onehot_of(j % 2, u + 2, L0 + u + 1)
                    dve.wait_ge(gu_done, E0 + u + 1)
                    dve.wait_ge(silu_ready, E0 + u + 1)
                    dve.wait_ge(list_ready, L0 + u + 1)
                    STT(hid[:, :], ps[:, 2, DE:2 * DE], cw[j][:, :], sg[:, :], ALU.mult, ALU.mult).then_inc(hid_ready, 1)
                    wait_any(dve, scattered[j % 2], S0 + 32 * r + 16 * (j // 2))
                    list_of((j + 2) % 4, L0 + u + 3)
                    xgt_copy((j + 1) % 2, T0 + u + 2)
                    if j or not isinstance(u, int):
                        rows_out(u - 1, (j - 1) % 2, 32 * r + 16 * ((j - 1) // 2))

                experts_in_order(dve, expert, NEXP)
                rows_out(NEXP - 1, 1, 16 * (NEXP // 2 - 1))

            def next_slots(ps_no):
                dve.wait_ge(onehot_ready, ps_no * NU)
                dve.wait_ge(list_done, ps_no * NU)
                nc.vector.tensor_scalar(slot_no[:, :], slot_no[:, :], float(P), None, ALU.add).then_inc(slots_moved, 1)
                dve.wait_ge(slots_moved, ps_no)

            experts_of_pass(0)
            with dve.If(dve.value_load(load_max[0:1, 0:1], min_val=0, max_val=SEQ) > P):
                with dve.Fori(1, NT) as ps_no:
                    next_slots(ps_no)
                    experts_of_pass(ps_no, again=True)
            nc.vector.memset(mark[:, 2:3], 0.0).then_inc(experts_over, 1)

            G, S = 2 * NCHUNK, 8 * NCHUNK

            def lo_tail(n):
                s = n % 2
                dve.wait_ge(hi_ready, G + n + 1)
                TT(w_l[s][:, :, :], raw[s][:, :, :], w_h[s][:, :, :].bitcast(F32), ALU.subtract).then_inc(lo_ready, 1)

            lo_tail(0)
            for k in range(2):
                dve.wait_ge(ph_ready, k + 1)
                TT(pT_l[:, k, :], aux[:, k, :], pT_h[:, k, :].bitcast(F32), ALU.subtract).then_inc(pl_ready, 1)
            dve.wait_ge(bpg_landed, 16)
            lo_tail(1)
            lo_tail(2)
            for c in range(2):
                for t in range(NT):
                    dve.wait_ge(slice_done, S + 8 * c + 5 + t)
                    TT(sgp[:, t, c * W:(c + 1) * W], ps[:, t, :], bias_bc[0][:, c * W:(c + 1) * W], ALU.add).then_inc(pg_read, 1)
                if c == 0:
                    lo_tail(3)
                    lo_tail(4)
            lo_tail(5)
            for t in range(NT):
                for c in range(2):
                    n = 2 * t + c
                    if n == 4:
                        lo_tail(6)
                    cols_ = slice(c * W, (c + 1) * W)
                    dve.wait_ge(slice_done, S + 16 + (n // 2) + 1)
                    dve.wait_ge(pg_ready, 8)
                    TT(sgp[:, t, cols_], aux[:, n % 4, :], sgp[:, t, cols_], ALU.mult).then_inc(wp_read, 1)
                    dve.wait_ge(wp_read, n + 1)
                    STT(xres[:, t, cols_], xres[:, t, cols_], ALPHA, sgp[:, t, cols_], ALU.mult, ALU.add).then_inc(wp_added, 1)

            def sum_rows(t):
                y = yt[t % 2]
                dve.wait_ge(y_landed[t % 2], 16 * (t // 2 + 1))
                for n in (4, 2, 1):
                    step.link(TT(y[:, 0:n, :], y[:, 0:n, :], y[:, n:2 * n, :], ALU.add))
                if t == 0:
                    dve.wait_ge(wp_added, 8)
                TT(xres[:, t, :], xres[:, t, :], y[:, 0, :], ALU.add).then_inc(y_summed, 1)

            sum_rows(0)
            lo_tail(7)
            for t in range(NT):
                dve.wait_ge(sh_silu, t + 1)
                TT(hs[:, t, :], ps[:, t, DE:2 * DE], sg_s[:, t, :], ALU.mult).then_inc(sh_ready, 1)
            for k in range(2):
                dve.wait_ge(hh_ready, k + 1)
                TT(hsT_l[:, k, :], aux[:, k, :], hsT_h[:, k, :].bitcast(F32), ALU.subtract).then_inc(hl_ready, 1)
            sum_rows(1)
            sum_rows(2)
            sum_rows(3)
            dve.wait_ge(ln2_landed, 32)
            dve.wait_ge(y_summed, NT)
            for t in range(NT):
                for c in range(2):
                    n = 2 * t + c
                    dve.wait_ge(slice_done, S + 28 + (n // 2) + 1)
                    TT(xres[:, t, c * W:(c + 1) * W], xres[:, t, c * W:(c + 1) * W], (aux if n % 8 < 4 else ps)[:, n % 4, :],
                       ALU.add).then_inc(ds_added, 1)
                dve.wait_ge(ds_added, 2 * t + 2)
                norm(t, stat3, mv3, rstd3, var3_ready, std3_ready, t + 1, out_ready)

        @block.tensor
        def _(pe):
            mm = nc.tensor.matmul

            def product(bank, halves, k, t, first, last):
                (a_h, a_l), (b_h, b_l) = halves
                mm(bank, a_h, b_h, start=first, stop=False)
                mm(bank, a_h, b_l, start=False, stop=False)
                return mm(bank, a_l, b_h, start=False, stop=last)

            pe.wait_ge(const_ready, 7)
            for k in range(NK):
                if k >= 4:
                    pe.wait_ge(xl_ready, k - 3)
                for t in range(NT):
                    if k == 0:
                        pe.wait_ge(x_landed[t], 16)
                    ins = nc.tensor.transpose(aux[:, k % 4, t * P:(t + 1) * P], x_in[:, t, k * P:(k + 1) * P], ident[:, :])
                ins.then_inc(xt_done, 1)
            pe.wait_ge(vec_landed, 16 * 9)
            pe.wait_ge(xl_ready, 8)
            nc.tensor.transpose(aux[:, 1, 0:NROW], vec[:, :], ident[0:NROW, 0:NROW]).then_inc(vec_done, 1)
            pe.wait_ge(gw_lo, 1)
            for k in range(NK):
                ins = product(aux[:, 0, :], ((wg_h[:, k, :], wg_l[:, k, :]), (xT_h[:, k, :], xT_l[:, k, :])), k, 0,
                              k == 0, k == NK - 1)
            ins.then_inc(gates_done, 1)
            pe.wait_ge(ws_landed, 16)
            for g in range(GG):
                ins = nc.tensor.transpose(aux[:, 2 + g // 4, (g % 4) * P:(g % 4 + 1) * P], ws_in[:, g, :], ident[:, :])
                if g % 4 == 3:
                    ins.then_inc(wst_done, 1)

            def token_columns():
                pe.wait_ge(rows_ready, 4)
                pe.wait_ge(wst_ready, 1)
                pe.wait_ge(bcol_ready, 1)
                for h in range(MH):
                    ins = mm(aux[:, 0, h * NC:(h + 1) * NC], sel[:, h, :], dec_row[:, :], start=True, stop=True)
                ins.then_inc(cols_done, 1)
                for t in range(NT):
                    for n, r in enumerate((r_a, r_f, r_em)):
                        at = t * 3 * MH + n * MH
                        ins = nc.tensor.transpose(aux[:, 1, at:at + MH], r[:, t * P:(t + 1) * P], ident[0:MH, 0:MH])
                ins.then_inc(cols_done, 1)
                for g in range(2):
                    mm(aux[:, 2 + g, :], ones[:, :], wsT[:, 4 * g:4 * g + 4, :].rearrange("p g t -> p (g t)"),
                       start=True, stop=True).then_inc(rsum_done, 1)

            def head_inputs(h):
                kT, qT = qkT[:, 1, h, :], qkT[:, 0, h, :]
                if h == 0:
                    pe.wait_ge(drained, drains("qk"))
                    pe.wait_ge(cols_ready, 2)
                    pe.wait_ge(rsum_read, GG)
                else:
                    pe.wait_ge(num_read, NT * h)
                for t in range(NT):
                    at = slice(t * P, (t + 1) * P)
                    ins = mm(aux[:, 0, at], kT[:, at], qT[:, at], start=True, stop=True)
                ins.then_inc(a_done, 1)
                mm(aux[:, 1, :], sel[:, h, :], u_row[:, :], start=True, stop=True).then_inc(a_done, 1)
                mm(aux[:, 2, :], sel[:, h, :], win_row[:, :], start=True, stop=True).then_inc(a_done, 1)
                for t in range(NT):
                    at = slice(t * P, (t + 1) * P)
                    ins = nc.tensor.transpose(aux[:, 3, at], kT[:, at], ident[:, :])
                ins.then_inc(a_done, 1)

            def head_products(h):
                pe.wait_ge(head_ready, 4 * h + 4)
                pe.wait_ge(drained, drains("vm"))
                for c in range(NC - 1):
                    if c >= 4:
                        pe.wait_ge(state_ready, (NC - 1) * h + c - 3)
                    t, at = c // 2, slice((c % 2) * CHUNK, (c % 2 + 1) * CHUNK)
                    mm(aux[:, c % 4, 0:MVE], kw[at, t, :], vme[at, t, h, :], start=True, stop=True).then_inc(kv_done, 1)
                for t in range(NT):
                    pe.wait_ge(state_ready, (NC - 1) * h + (5, 6, 7, 7)[t])
                    bank = aux[:, t, 0:MVE]
                    mm(bank, wS[:, t, :], vme[:, t, h, :], start=True, stop=False)
                    mm(bank, q_pad[:, t, 0, :], state[:, 2 * t, :], start=False, stop=False)
                    mm(bank, q_pad[:, t, 1, :], state[:, 2 * t + 1, :], start=False, stop=True).then_inc(num_done, 1)

            moving = {"pa": (aT_h, aT_l), "pb": (mT_h, mT_l), "out": (yT_h, yT_l)}
            for n, kind in enumerate(KINDS):
                c0 = first_chunk[kind]
                m_h, m_l = moving.get(kind, (xT_h, xT_l))
                if kind == "pa":
                    pe.wait_ge(al_ready, GG)
                if kind == "pb":
                    pe.wait_ge(ml_ready, NK)
                if kind == "out":
                    pe.wait_ge(yl_ready, NK)

                def chunk(i):
                    for s in range(2):
                        pe.wait_ge(lo_ready, 2 * (c0 + i) + s + 1)
                        for t in range(4):
                            if s == 0 and not (kind == KINDS[0] and isinstance(i, int) and i == 0):
                                pe.wait_ge(drained, 4 * (c0 + i) - 3 + t)
                            for kk in range(HK):
                                k = s * HK + kk
                                at = slice(t * P, (t + 1) * P)
                                if kind in FEATURE:
                                    halves = ((w_h[s][:, kk, at], w_l[s][:, kk, at]), (m_h[:, k, :], m_l[:, k, :]))
                                else:
                                    halves = ((m_h[:, k, at], m_l[:, k, at]), (w_h[s][:, kk, :], w_l[s][:, kk, :]))
                                ins = product(ps[:, t, :], halves, k, t, k == 0, k == NK - 1)
                            ins.then_inc(slice_done, 1)

                if kind == KINDS[0]:
                    chunk(0)
                    chunk(1)
                else:
                    with pe.Fori(0, 2) as i:
                        chunk(i)
                if kind == "vm":
                    token_columns()
                    head_inputs(0)
                if kind == "v":
                    head_products(0)
                    head_inputs(1)
                if kind == "u":
                    pe.wait_ge(vn_ready, NT)
                    pe.wait_ge(head_ready, 8)
                    for g in range(GG):
                        if g >= 4:
                            pe.wait_ge(mixed_read, g - 3)
                        for t in range(NT):
                            ins = mm(aux[:, g % 4, t * P:(t + 1) * P], v_sb[:, t, g * P:(g + 1) * P], wsT[:, g, :],
                                     start=True, stop=True)
                        ins.then_inc(mixed_done, 1)
                    pe.wait_ge(mixed_read, GG)
                    head_products(1)
                    head_inputs(2)
                if kind == "ga":
                    head_products(2)
                    head_inputs(3)
                if kind == "pa":
                    head_products(3)
                if kind == "o":
                    pe.wait_ge(mb_ready, NT * MH)
                    pe.wait_ge(num_read, NT * MH)
                    for k in range(NK):
                        if k >= 4:
                            pe.wait_ge(ml_ready, k - 3)
                        for t in range(NT):
                            ins = nc.tensor.transpose(aux[:, k % 4, t * P:(t + 1) * P], osig[:, t, k * P:(k + 1) * P],
                                                      ident[:, :])
                        ins.then_inc(mt_done, 1)

            def route(t):
                pe.wait_ge(x1l_ready, 2 * t + 2)
                at = slice(t * P, (t + 1) * P)
                for k in range(NK):
                    ins = product(ps[:, 0, t * NEXP:(t + 1) * NEXP], ((x1T_h[:, k, at], x1T_l[:, k, at]),
                                                                      (wr_h[:, k, :], wr_l[:, k, :])), k, t,
                                  k == 0, k == NK - 1)
                ins.then_inc(router_done, 1)

            for t in range(NT):
                pe.wait_ge(x1_ready, t + 1)
                for n in range(2):
                    b = 2 * t + n
                    if b >= 4:
                        pe.wait_ge(x1l_ready, b - 3)
                    for kk in range(HK):
                        k = n * HK + kk
                        ins = nc.tensor.transpose(aux[:, b % 4, kk * P:(kk + 1) * P], xres[:, t, k * P:(k + 1) * P],
                                                  ident[:, :])
                    ins.then_inc(x1t_done, 1)
                if t == 0:
                    pe.wait_ge(wr_lo, 1)
                else:
                    route(t - 1)
            route(NT - 1)
            pe.wait_ge(chosen_ready, 1)
            pe.wait_ge(route_const, 1)
            for t in range(NT):
                bank = ps[:, 1, t * NEXP:(t + 1) * NEXP]
                for s in range(t):
                    mm(bank, ones[:, :], chosen[:, s, :], start=(s == 0), stop=False)
                mm(bank, before[:, :], chosen[:, t, :], start=(t == 0), stop=True).then_inc(pos_done, 1)
            for t in range(NT):
                ins = mm(ps[:, 2, 0:NEXP], ones[:, :], chosen[:, t, :], start=(t == 0), stop=(t == NT - 1))
            ins.then_inc(pos_done, 1)

            def list_of(n, e, count):
                pe.wait_ge(onehot_ready, count)
                at = 4 * (n % 2)
                for t in range(NT):
                    ins = mm(ps[:, 3, at:at + 3], onehot[n % 2][:, t, :],
                             table[:, t, bass.ds(e, 1), :].rearrange("p e c -> p (e c)"), start=(t == 0), stop=(t == NT - 1))
                ins.then_inc(list_done, 1)

            def transposes(n, landed):
                pe.wait_ge(gathered[n], landed)
                for k in range(NK):
                    ins = nc.tensor.transpose(ps[:, k // HK, (k % HK) * P:(k % HK + 1) * P], xg[n][:, k:D:NK], ident[:, :])
                ins.then_inc(xgt_done, 1)

            def experts_of_pass(ps_no):
                T0, E0, L0 = ps_no * (NEXP + 1), ps_no * NEXP, ps_no * NU
                R0, W0 = ps_no * (16 * NU // 2), ps_no * (NEXP // 4)
                list_of(0, 0, L0 + 1)
                pe.wait_ge(list_ready, L0 + 1)
                list_of(1, 1, L0 + 2)
                transposes(0, R0 + 16)

                def down(v, j, r):
                    pe.wait_ge(hidt_ready, E0 + v + 1)
                    pe.wait_ge(dn_landed[j], 16 * (W0 + r + 1))
                    wait_any(pe, y_act, E0 + v)
                    wait_any(pe, y_dve, E0 + v)
                    for c in range(2):
                        for k in range(2):
                            ins = mm(aux[:, 2 + c, :], hidT[:, k, :], dn[j][:, k, c * W:(c + 1) * W], start=(k == 0),
                                     stop=(k == 1))
                    ins.then_inc(dn_done, 1)

                def expert(u, j, r):
                    pe.wait_ge(xgt_act, T0 + u + 1)
                    pe.wait_ge(xgt_dve, T0 + u + 1)
                    pe.wait_ge(gu_landed[j], 32 * (W0 + r + 1))
                    for k in range(NK):
                        ins = mm(ps[:, 2, :], xgT[j % 2][:, k, :], gu[j][:, k, :], start=(k == 0), stop=(k == NK - 1))
                    ins.then_inc(gu_done, 1)
                    pe.wait_ge(list_ready, L0 + u + 2)
                    list_of(j, u + 2, L0 + u + 3)
                    transposes((j + 1) % 2, R0 + 32 * r + 16 * ((j + 1) // 2) + 16)
                    if j:
                        down(u - 1, j - 1, r)
                    elif not isinstance(u, int):
                        down(u - 1, 3, r - 1)
                    pe.wait_ge(hid_ready, E0 + u + 1)
                    for k in range(2):
                        ins = nc.tensor.transpose(aux[:, 0, k * P:(k + 1) * P], hid[:, k:DE:2], ident[:, :])
                    ins.then_inc(hidt_done, 1)

                experts_in_order(pe, expert, NEXP)
                down(NEXP - 1, 3, NEXP // 4 - 1)
                pe.wait_ge(y_act, E0 + NEXP)
                pe.wait_ge(y_dve, E0 + NEXP)
                pe.wait_ge(list_ready, L0 + NU)
                pe.wait_ge(xgt_act, T0 + NEXP + 1)
                pe.wait_ge(xgt_dve, T0 + NEXP + 1)

            pe.wait_ge(table_ready, 1)
            experts_of_pass(0)
            pe.wait_ge(load_ready, 1)
            with pe.If(pe.value_load(load_max[0:1, 0:1], min_val=0, max_val=SEQ) > P):
                with pe.Fori(1, NT) as ps_no:
                    experts_of_pass(ps_no)

            pe.wait_ge(p_landed, 16)
            for k in range(2):
                for t in range(NT):
                    ins = nc.tensor.transpose(aux[:, k, t * P:(t + 1) * P], p_in[:, t, k * P:(k + 1) * P], ident[:, :])
                ins.then_inc(pt_done, 1)
            G = 2 * NCHUNK

            def whole(g0, read_sem, read0):
                for s in range(2):
                    w = (g0 + s) % 2
                    pe.wait_ge(lo_ready, G + g0 + s + 1)
                    for t in range(NT):
                        if s == 0 and read_sem is not None:
                            pe.wait_ge(read_sem, read0 + t + 1)
                        at = slice(t * P, (t + 1) * P)
                        for kk in range(HK):
                            k = s * HK + kk
                            ins = product(ps[:, t, :], ((x1T_h[:, k, at], x1T_l[:, k, at]),
                                                        (w_h[w][:, kk, :], w_l[w][:, kk, :])), k, t, k == 0, k == NK - 1)
                        ins.then_inc(slice_done, 1)

            def short(g, f_h, f_l, banks, read_sem=None):
                pe.wait_ge(lo_ready, G + g + 1)
                rows = lambda w: w[g % 2][:, :, :].rearrange("p (k a) n -> p k (a n)", k=2)
                for t in range(NT):
                    at = slice(t * P, (t + 1) * P)
                    for c in range(2):
                        n = 2 * t + c
                        if read_sem is not None and n >= 4:
                            pe.wait_ge(read_sem, n - 3)
                        for k in range(2):
                            cols_ = slice(c * W, (c + 1) * W)
                            ins = product(banks(n), ((f_h[:, k, at], f_l[:, k, at]),
                                                     (rows(w_h)[:, k, cols_], rows(w_l)[:, k, cols_])), k, t, k == 0, k == 1)
                    ins.then_inc(slice_done, 1)

            whole(0, None, 0)
            whole(2, pg_read, 0)
            pe.wait_ge(pl_ready, 2)
            short(4, pT_h, pT_l, lambda n: aux[:, n % 4, :], wp_read)
            whole(5, pg_read, 4)
            pe.wait_ge(sh_ready, NT)
            pe.wait_ge(wp_read, 8)
            for k in range(2):
                for t in range(NT):
                    ins = nc.tensor.transpose(aux[:, k, t * P:(t + 1) * P], hs[:, t, k * P:(k + 1) * P], ident[:, :])
                ins.then_inc(ht_done, 1)
            pe.wait_ge(hl_ready, 2)
            short(7, hsT_h, hsT_l, lambda n: (aux if n < 4 else ps)[:, n % 4, :])


IN_NAMES = ["x", "p", "w_in", "b_in", "sg_ln_g", "sg_ln_b", "w_s", "b_s", "mh_g", "w_pa", "w_pb", "w_out",
            "ln1_g", "ln1_b", "w_router", "b_router", "w_gate_e", "w_up_e", "w_down_e",
            "w_gate_s", "w_up_s", "w_down_s", "w_pg", "b_pg", "w_p", "ln2_g", "ln2_b"]


def kernel(**inputs):
    import numpy as _np
    import concourse.bacc as _bacc
    from concourse import mybir as _mybir
    from concourse.bass_utils import run_bass_kernel_spmd as _run

    nc = _bacc.Bacc("TRN2", target_bir_lowering=False, num_devices=1)
    arrays, aps = {}, {}
    for name in IN_NAMES:
        a = _np.ascontiguousarray(inputs[name])
        a = a[0]
        if name == "p":
            a = a[0]
        arrays[f"in_{name}"] = a
        aps[name] = nc.dram_tensor(f"in_{name}", a.shape, _mybir.dt.from_np(a.dtype), kind="ExternalInput").ap()
    out = nc.dram_tensor("out", (SEQ, D), _mybir.dt.float32, kind="ExternalOutput").ap()
    build(nc, aps, out)
    r = _run(nc, [arrays], core_ids=[0])
    return r.results[0]["out"].reshape(1, SEQ, D)
```

```python
import concourse.bass as bass
from concourse import mybir
from contextlib import ExitStack
import math

F32 = mybir.dt.float32
F32R = mybir.dt.float32r
BF16 = mybir.dt.bfloat16
I32 = mybir.dt.int32
U32 = mybir.dt.uint32
ALU = mybir.AluOpType
ACT = mybir.ActivationFunctionType
AX = mybir.AxisListType

P = 128
D = 1024
SEQ = 512
NT = SEQ // P
NK = D // P
CHUNK = 64
NC = SEQ // CHUNK
GW, GG = 1024, 8
MH, QK, MV = 4, 128, 256
MVE = MV + 1
NEXP, TOPK, NGRP, TOPG = 64, 8, 8, 4
DE = 256
ROUTE_SCALE = 2.5
DEPTH = 1
ALPHA = (2 * DEPTH) ** 0.25
LN_EPS, RMS_EPS = 1e-5, 1e-6
BIG_NEG = -1.0e30

C_U, C_V = 0, GW
C_Q = 2 * GW
C_K = C_Q + MH * QK
C_VM = C_K + MH * QK
C_O = C_VM + MH * MV
C_I = C_O + MH * MV
C_F = C_I + MH
C_GA = C_F + MH
C_GB = C_GA + D
W = 512
HK = NK // 2


class Count:

    def __init__(self, eng, sem):
        self.eng, self.sem, self.base, self.more = eng, sem, 0, 0

    def inc(self, ins):
        ins.then_inc(self.sem, 1)
        self.more += 1
        return ins

    def link(self, ins):
        self.inc(ins)
        self.eng.wait_ge(self.sem, self.base + self.more)


def wait_any(eng, s, value):
    if not (isinstance(value, int) and value == 0):
        eng.wait_ge(s, value)


def experts_in_order(eng, expert, n):
    for u in range(4):
        expert(u, u, 0)
    with eng.Fori(1, n // 4) as i:
        for j in range(4):
            expert(4 * i + j, j, i)


def build(nc, A, out):
    ctx = ExitStack()
    with ctx:
        def sem(name):
            return ctx.enter_context(nc.semaphore(name))

        ARENA = -(-nc.sbuf_base // 64) * 64

        def sb(name, shape, dt, at):
            return nc.alloc_sbuf_tensor_at(name, shape, dt, offset=ARENA + at)

        KB = 1024
        at_xh, at_xl, at_raw, at_split = 0, 16 * KB, 32 * KB, (48 * KB, 64 * KB)
        at_r1, at_r2, at_r3, at_r4, at_r5 = 80 * KB, 96 * KB, 112 * KB, 128 * KB, 144 * KB
        at_small = at_r5 + 4 * NT * MH * MVE
        xT_h = sb("xT_h", [P, NK, SEQ], F32R, at_xh)
        xT_l = sb("xT_l", [P, NK, SEQ], F32R, at_xl)
        yT_h = sb("yT_h", [P, NK, SEQ], F32R, at_xh)
        yT_l = sb("yT_l", [P, NK, SEQ], F32R, at_xl)
        raw = [sb(f"raw{s}", [P, HK, W], F32, at_raw + 8 * KB * s) for s in range(2)]
        w_h = [sb(f"w_h{s}", [P, HK, W], F32R, at_split[s]) for s in range(2)]
        w_l = [sb(f"w_l{s}", [P, HK, W], F32R, at_split[s] + 8 * KB) for s in range(2)]
        qkT = sb("qkT", [P, 2, MH, SEQ], F32, at_r1)
        osig = sb("osig", [P, NT, D], F32, at_r1)
        xres = sb("xres", [P, NT, D], F32, at_r1)
        x_in = sb("x_in", [P, NT, D], F32, at_r2)
        v_sb = sb("v_sb", [P, NT, GW], F32, at_r2)
        aT_h = sb("aT_h", [P, NK, SEQ], F32R, at_r2)
        mT_h = sb("mT_h", [P, NK, SEQ], F32R, at_r2)
        x1T_h = sb("x1T_h", [P, NK, SEQ], F32R, at_r2)
        ws_in = sb("ws_in", [P, GG, P], F32, at_r3)
        aT_l = sb("aT_l", [P, NK, SEQ], F32R, at_r3)
        mT_l = sb("mT_l", [P, NK, SEQ], F32R, at_r3)
        x1T_l = sb("x1T_l", [P, NK, SEQ], F32R, at_r3)
        row = [sb(f"row{n}", [MH, SEQ], F32, at_r4 + 2 * KB * n) for n in range(8)]
        r_f, r_t, r_a, r_b, r_cm, r_one, r_neg, r_em = row
        uT = sb("uT", [P, NK, SEQ], F32, at_r4)
        yT = sb("yT", [P, NK, SEQ], F32, at_r4)
        vme = sb("vme", [P, NT, MH, MVE], F32, at_r5)
        gbT = sb("gbT", [P, NK, SEQ], F32, at_r5)

        spot = [at_small]

        def small(name, shape, dt=F32):
            size = 4 * math.prod(shape[1:])
            t = sb(name, shape, dt, spot[0])
            spot[0] += -(-size // 32) * 32
            return t

        ident = small("ident", [P, P])
        ones = small("ones", [P, P])
        intra = small("intra", [P, P])
        sel = small("sel", [MH, MH, P])
        mark = small("mark", [P, 4])
        load_max = small("load_max", [P, 1], I32)
        eps_ln = small("eps_ln", [P, 1])
        bias_bc = [small(f"bias_bc{n}", [P, D]) for n in range(2)]
        at_ws = spot[0]
        wsT = small("wsT", [P, GG, P])
        add_bc = small("add_bc", [P, GG, P])
        at_state = spot[0]
        state = small("state", [P, NC, MVE])
        wg_h = sb("wg_h", [P, NK, P], F32R, at_state)
        wg_l = sb("wg_l", [P, NK, P], F32R, at_state + 4 * KB)
        kw = small("kw", [P, NT, P])
        q_pad = small("q_pad", [P, NT, 2, P])
        wS = small("wS", [P, NT, P])
        wexp = small("wexp", [P, NT, P])
        tmp = small("tmp", [P, W])
        wg_raw = sb("wg_raw", [P, NK, P], F32, at_r3 + 4 * KB)
        u_row = small("u_row", [MH, SEQ])
        win_row = small("win_row", [MH, SEQ])
        cols = small("cols", [P, NT, 3 * MH])
        dec_row = small("dec_row", [MH, NC])
        dec_bc = small("dec_bc", [P, MH, NC])
        m_row = small("m_row", [MH, NC + 1])
        g_row = small("g_row", [MH, NC])
        bif = small("bif", [MH, 2])
        NROW = 7 * NK
        vec = sb("vec", [NROW, P], F32, at_r3 + 8 * KB)
        bcol = small("bcol", [P, NROW])
        B_QK, B_U, B_GA, B_GB, B_SG, B_SB, B_MG = range(0, NROW, NK)
        stat = small("stat", [P, NT, 2, 6])
        mv = small("mv", [P, NT, 2])
        rstd = small("rstd", [P, NT])
        eps_rms = small("eps_rms", [P, 1])
        den = small("den", [P, NT, MH])
        ssq = small("ssq", [P, NT, MH])
        hsc = small("hsc", [P, NT, MH])
        hs2 = small("hs2", [P, NT, MH])
        junk = small("junk", [P, MV])
        x1_rows = nc.dram_tensor("x1_rows", [SEQ, D], F32).ap()
        y_rows = nc.dram_tensor("y_rows", [SEQ * TOPK, D], F32).ap()
        gu = [sb(f"gu{j}", [P, NK, 2 * DE], F32, at) for j, at in
              enumerate((at_r4, at_raw, at_split[1], at_split[0]))]
        dn = [sb(f"dn{j}", [P, 2, D], F32, at) for j, at in
              enumerate((0, 8 * KB, at_r5, at_r5 + 8 * KB))]
        xg = [sb(f"xg{n}", [P, D], F32, (16 + 4 * n) * KB) for n in range(2)]
        xgT = [sb(f"xgT{n}", [P, NK, P], F32, (24 + 4 * n) * KB) for n in range(2)]
        spot2 = [at_small + 8 * P]

        def small2(name, shape, dt=F32):
            size = (2 if dt == BF16 else 4) * math.prod(shape[1:])
            t = sb(name, shape, dt, spot2[0])
            spot2[0] += -(-size // 32) * 32
            return t

        assert spot2[0] <= at_small + 2 * 4 * P
        NU = NEXP + 2
        before = small2("before", [P, P])
        spot2[0] = at_ws
        wr_raw = small2("wr_raw", [P, NK, NEXP])
        br_bc = small2("br_bc", [P, NEXP])
        slot_no = small2("slot_no", [P, P])
        p_in = sb("p_in", [P, NT, 2 * P], F32, spot2[0])
        onehot = [small2(f"onehot{n}", [P, NT, P], BF16) for n in range(2)]
        scores = small2("scores", [P, NT, NEXP])
        chosen = small2("chosen", [P, NT, NEXP])
        pos = small2("pos", [P, NT, NU])
        NLIST = 6
        table = small2("table", [P, NT, NU, NLIST], BF16)
        rtmp = small2("rtmp", [P, NT, NEXP])
        at_y = spot2[0]
        sel8 = small2("sel8", [P, NT, NGRP, 8])
        grp = small2("grp", [P, NT, NGRP])
        gtop = small2("gtop", [P, NT, 8])
        gidx = small2("gidx", [P, NT, 8], U32)
        gidf = small2("gidf", [P, NT, 8])
        geq = small2("geq", [P, NT, 8])
        gmask = small2("gmask", [P, NT, 8])
        iota8 = small2("iota8", [P, 8])
        etop = small2("etop", [P, NT, 8])
        wsum = small2("wsum", [P, NT])
        in_tile = small2("in_tile", [P, 1])
        tile_no = small2("tile_no", [P, NT])
        cmax = small2("cmax", [P, 1])
        spot2[0] = at_y
        y_sb = [small2(f"y_sb{n}", [P, D]) for n in range(2)]
        pT_h = sb("pT_h", [P, 2, SEQ], F32R, at_y + 4 * KB)
        pT_l = small2("pT_l", [P, 2, SEQ], F32R)
        spot2[0] = max(spot2[0], at_y + 8 * KB)
        sg = small2("sg", [P, DE])
        hid = small2("hid", [P, DE])
        hidT = small2("hidT", [P, 2, P])
        ixg = [small2(f"ixg{n}", [P, 1], U32) for n in range(4)]
        ixs = [small2(f"ixs{n}", [P, 1], U32) for n in range(4)]
        cw = [small2(f"cw{n}", [P, 1]) for n in range(4)]
        list_parts = small2("list_parts", [P, NLIST])
        list_token = small2("list_token", [P, 1])
        list_row = small2("list_row", [P, 1])
        list_weight = small2("list_weight", [P, 1])
        stat2 = small2("stat2", [P, NT, 2, 6])
        mv2 = small2("mv2", [P, NT, 2])
        rstd2 = small2("rstd2", [P, NT])
        off2 = small2("off2", [P, NT])
        assert ARENA + spot2[0] <= nc.sbuf_usable_end, (ARENA + spot2[0], nc.sbuf_usable_end)
        emb = [sb(f"emb{c}", [P, NT, W], F32, at) for c, at in enumerate((at_r5, 0))]
        emb_rows = nc.dram_tensor("emb_rows", [SEQ, W], F32).ap()
        sgp = [sb("sgp0", [P, NT, W], F32, at_r5 + 8 * KB)]
        yt = [sb(f"yt{n}", [P, TOPK, D], F32, at) for n, at in enumerate((at_r4, 0, at_r2))]
        spot2[0] = at_ws
        sg_s = small2("sg_s", [P, NT, DE])
        hs = small2("hs", [P, NT, DE])
        hsT_h = small2("hsT_h", [P, 2, SEQ], F32R)
        hsT_l = small2("hsT_l", [P, 2, SEQ], F32R)
        sgp.append(small2("sgp1", [P, NT, W]))
        emb_again = small2("emb_again", [P, NT, W])
        stat3 = small2("stat3", [P, NT, 2, 6])
        mv3 = small2("mv3", [P, NT, 2])
        rstd3 = small2("rstd3", [P, NT])
        off3 = small2("off3", [P, NT])
        assert ARENA + spot2[0] <= nc.sbuf_usable_end
        NOWHERE = 4 * NT

        assert ARENA + spot[0] <= nc.sbuf_usable_end, (ARENA + spot[0], nc.sbuf_usable_end)

        ps = ctx.enter_context(nc.psum_tensor("ps", [P, 4, W], F32))
        aux = ctx.enter_context(nc.psum_tensor("aux", [P, 4, W], F32))

        def tiles(bank):
            return aux[:, bank, :].rearrange("p (t c) -> p t c", t=NT)

        YS, YH = 608, 304

        def over_free(col, shape):
            return col.unsqueeze(len(shape) - 1).to_broadcast(shape)

        KINDS = ["qk", "vm", "v", "u", "ga", "pa", "o", "gb", "pb", "out"]
        FEATURE = {"qk", "u", "ga", "pa", "gb", "pb"}
        source = {"qk": (A["w_in"], C_Q), "vm": (A["w_in"], C_VM), "v": (A["w_in"], C_V),
                  "u": (A["w_in"], C_U), "ga": (A["w_in"], C_GA), "pa": (A["w_pa"], 0),
                  "o": (A["w_in"], C_O), "gb": (A["w_in"], C_GB), "pb": (A["w_pb"], 0),
                  "out": (A["w_out"], 0)}
        first_chunk = {k: 2 * n for n, k in enumerate(KINDS)}
        NCHUNK = 2 * len(KINDS)
        G, S, R = 2 * NCHUNK, 8 * NCHUNK, 16 * NCHUNK

        x_landed = [sem(f"x_landed{t}") for t in range(NT)]
        const_ready = sem("const_ready")
        gate_w_landed = sem("gate_w_landed")
        vec_landed = sem("vec_landed")
        ws_landed = sem("ws_landed")
        bs_landed = sem("bs_landed")
        bias_landed = [sem(f"bias_landed{n}") for n in range(5)]
        xres_landed = sem("xres_landed")
        raw_landed = [sem(f"raw_landed{s}") for s in range(2)]
        hi_ready = sem("hi_ready")
        lo_ready = sem("lo_ready")
        slice_done = sem("slice_done")
        drained = sem("drained")

        def drains(kind, chunk=1, t=3):
            return 4 * (first_chunk[kind] + chunk) + t + 1

        act_step = sem("act_step")
        dve_step = sem("dve_step")
        pool_step = sem("pool_step")
        xt_done = sem("xt_done")
        xh_ready = sem("xh_ready")
        xl_ready = sem("xl_ready")
        gw_hi = sem("gw_hi")
        gw_lo = sem("gw_lo")
        gates_done = sem("gates_done")
        gates_read = sem("gates_read")
        gate_abs = sem("gate_abs")
        gate_log = sem("gate_log")
        exp_asked = sem("exp_asked")
        vec_done = sem("vec_done")
        bcol_ready = sem("bcol_ready")
        wst_done = sem("wst_done")
        wst_ready = sem("wst_ready")
        rows_ready = sem("rows_ready")
        cols_done = sem("cols_done")
        cols_ready = sem("cols_ready")
        a_done = sem("a_done")
        arg_ready = sem("arg_ready")
        wexp_ready = sem("wexp_ready")
        wmask_ready = sem("wmask_ready")
        head_ready = sem("head_ready")
        kv_done = sem("kv_done")
        state_ready = sem("state_ready")
        num_done = sem("num_done")
        num_den = sem("num_den")
        num_read = sem("num_read")
        v_ready = sem("v_ready")
        o_ready = sem("o_ready")
        var_ready = sem("var_ready")
        std_ready = sem("std_ready")
        vn_ready = sem("vn_ready")
        rsum_done = sem("rsum_done")
        rsum_read = sem("rsum_read")
        mixed_read = sem("mixed_read")
        mixed_done = sem("mixed_done")
        a_ready = sem("a_ready")
        ah_ready = sem("ah_ready")
        al_ready = sem("al_ready")
        ms_ready = sem("ms_ready")
        rms_ready = sem("rms_ready")
        mb_ready = sem("mb_ready")
        mt_done = sem("mt_done")
        mh_ready = sem("mh_ready")
        ml_ready = sem("ml_ready")
        yh_ready = sem("yh_ready")
        yl_ready = sem("yl_ready")
        y_ready = sem("y_ready")

        wr_landed = sem("wr_landed")
        stat2_ready = sem("stat2_ready")
        var2_ready = sem("var2_ready")
        std2_ready = sem("std2_ready")
        coef2_ready = sem("coef2_ready")
        centred2 = sem("centred2")
        x1_left = sem("x1_left")
        x1_right = sem("x1_right")
        x1_stored = sem("x1_stored")
        x1t_done = sem("x1t_done")
        x1h_ready = sem("x1h_ready")
        x1l_ready = sem("x1l_ready")
        router_done = sem("router_done")
        scores_ready = sem("scores_ready")
        route_const = sem("route_const")
        chosen_ready = sem("chosen_ready")
        pos_done = sem("pos_done")
        slots_moved = sem("slots_moved")
        table_ready = sem("table_ready")
        load_ready = sem("load_ready")
        gu_landed = [sem(f"gu_landed{j}") for j in range(4)]
        dn_landed = [sem(f"dn_landed{j}") for j in range(4)]
        onehot_ready = sem("onehot_ready")
        list_done = sem("list_done")
        list_step = sem("list_step")
        list_ready = sem("list_ready")
        rows_listed = sem("rows_listed")
        gathered = [sem(f"gathered{n}") for n in range(2)]
        xgt_done = sem("xgt_done")
        xgt_act = sem("xgt_act")
        xgt_dve = sem("xgt_dve")
        gu_done = sem("gu_done")
        silu_ready = sem("silu_ready")
        hid_ready = sem("hid_ready")
        hidt_done = sem("hidt_done")
        hidt_ready = sem("hidt_ready")
        dn_done = sem("dn_done")
        y_act = sem("y_act")
        y_dve = sem("y_dve")
        scattered = [sem(f"scattered{n}") for n in range(2)]
        routed_done = sem("routed_done")
        experts_over = sem("experts_over")
        bpg_landed = sem("bpg_landed")
        p_landed = sem("p_landed")
        pt_done = sem("pt_done")
        ph_ready = sem("ph_ready")
        pl_ready = sem("pl_ready")
        pg_read = sem("pg_read")
        pg_ready = sem("pg_ready")
        wp_read = sem("wp_read")
        gated = sem("gated")
        wp_added = sem("wp_added")
        emb_stored = sem("emb_stored")
        emb_back = sem("emb_back")
        sh_silu = sem("sh_silu")
        sh_ready = sem("sh_ready")
        ht_done = sem("ht_done")
        hh_ready = sem("hh_ready")
        hl_ready = sem("hl_ready")
        ds_added = sem("ds_added")
        ln2_landed = sem("ln2_landed")
        y_landed = [sem(f"y_landed{n}") for n in range(2)]
        y_last = [sem(f"y_last{c}") for c in range(2)]
        y_left = sem("y_left")
        y_right = sem("y_right")
        var3_ready = sem("var3_ready")
        std3_ready = sem("std3_ready")
        coef3_ready = sem("coef3_ready")
        centred3 = sem("centred3")
        out_left = sem("out_left")
        out_right = sem("out_right")
        out_stored = sem("out_stored")

        block = ctx.enter_context(nc.Block())

        def rows_of(w, half, col, n=W):
            return w[half * HK * P:(half + 1) * HK * P, bass.ds(col, n)].rearrange(
                "(k p) n -> p k n", p=P)

        @block.sync
        def _(sp):
            def wait_in_loop(s, value):
                value = sp.to_reg(value)
                sp.wait_ge(x_landed[0], 16)
                sp.wait_ge(s, value)

            for t in range(NT):
                sp.dma_start(x_in[:, t, :], A["x"][t * P:(t + 1) * P, :]).then_inc(x_landed[t], 16)
            for kind in KINDS:
                w, col = source[kind]
                c0 = first_chunk[kind]
                if kind == KINDS[0]:
                    for c in range(2):
                        for s in range(2):
                            if c:
                                sp.wait_ge(lo_ready, s + 1)
                            sp.dma_start(raw[s][:, :, :], rows_of(w, s, col + c * W)).then_inc(raw_landed[s], 16)
                    continue
                with sp.Fori(0, 2) as i:
                    for s in range(2):
                        wait_in_loop(lo_ready, 2 * c0 + s - 1 + i * 2)
                        sp.dma_start(raw[s][:, :, :], rows_of(w, s, col + i * W)).then_inc(raw_landed[s], 16)

            def gu_load(e, j):
                for n, w in enumerate(("w_gate_e", "w_up_e")):
                    sp.dma_start(gu[j][:, :, n * DE:(n + 1) * DE],
                                 A[w][bass.ds(e, 1)].rearrange("o (p k) f -> p (o k) f", k=NK)).then_inc(gu_landed[j], 16)

            def dn_load(e, j):
                sp.dma_start(dn[j][:, :, :], A["w_down_e"][bass.ds(e, 1)].rearrange("o (p k) f -> p (o k) f", k=2)
                             ).then_inc(dn_landed[j], 16)


            def extra_half(n, loads, wait=True):
                if wait:
                    sp.wait_ge(lo_ready, G + n - 1)
                for dst, src in loads:
                    sp.dma_start(dst, src).then_inc(raw_landed[n % 2], 16)

            def gate_half(n, wait=True):
                c, s = n // 2, n % 2
                extra_half(1 + n, [(raw[(1 + n) % 2][:, :, :], A["w_pg"][s * HK * P:(s + 1) * HK * P, c * W:(c + 1) * W
                                                                    ].rearrange("(k p) n -> p k n", p=P))], wait)

            extra_half(0, [(raw[0][:, :, :].rearrange("p (k a) n -> p k (a n)", k=2),
                            A["w_p"].rearrange("(k p) n -> p k n", p=P))])
            gate_half(0)

            def weights_of_pass(ps_no, first=False):
                if first:
                    sp.wait_ge(yl_ready, 8)
                gu_load(0, 0)
                if first:
                    gate_half(1)
                    sp.wait_ge(emb_stored, 16)
                dn_load(0, 0)
                if first:
                    sp.wait_ge(lo_ready, G + 3)
                gu_load(1, 1)
                dn_load(1, 1)
                if first:
                    sp.wait_ge(slice_done, S + 12)
                gu_load(2, 2)
                if first:
                    sp.wait_ge(slice_done, S + 16)
                gu_load(3, 3)
                if first:
                    sp.wait_ge(wp_added, NT)
                    sp.wait_ge(gathered[0], 32)
                dn_load(2, 2)
                dn_load(3, 3)
                with sp.Fori(0, NEXP // 4 - 1) as i:
                    for j in range(4):
                        wait_in_loop(gu_done, ps_no * NEXP + 4 * i + j + 1)
                        gu_load(4 * i + (4 + j), j)
                        wait_in_loop(dn_done, ps_no * NEXP + 4 * i + j + 1)
                        dn_load(4 * i + (4 + j), j)
                wait_in_loop(gu_done, (ps_no + 1) * NEXP - 2)

            weights_of_pass(0, first=True)
            sp.wait_ge(load_ready, 1)
            with sp.If(sp.value_load(load_max[0:1, 0:1], min_val=0, max_val=SEQ) > P):
                with sp.Fori(1, NT) as ps_no:
                    wait_in_loop(gu_done, ps_no * NEXP)
                    wait_in_loop(dn_done, ps_no * NEXP)
                    weights_of_pass(ps_no)
            gate_half(2, wait=False)
            gate_half(3, wait=False)
            for s in range(2):
                extra_half(5 + s, [(raw[(5 + s) % 2][:, :, n * DE:(n + 1) * DE],
                                    A[w][s * HK * P:(s + 1) * HK * P, :].rearrange("(k p) n -> p k n", p=P))
                                   for n, w in enumerate(("w_gate_s", "w_up_s"))])
            sp.wait_ge(routed_done, 1)
            sp.wait_ge(experts_over, 2)
            for t in range(NT - 1):
                if t >= 2:
                    sp.wait_ge(y_left, t - 1)
                    sp.wait_ge(y_right, t - 1)
                sp.dma_start(yt[t % 2][:, :, :], y_rows[t * P * TOPK:(t + 1) * P * TOPK, :].rearrange(
                    "(p k) d -> p k d", k=TOPK)).then_inc(y_landed[t % 2], 16)
                if t == 0:
                    sp.dma_start(emb_again[:, :, :], emb_rows.rearrange("(t p) n -> p t n", p=P)).then_inc(emb_back, 16)
                if t == 1:
                    extra_half(7, [(raw[1][:, :, :].rearrange("p (k a) n -> p k (a n)", k=2),
                                    A["w_down_s"].rearrange("(k p) n -> p k n", p=P))])
            sp.wait_ge(slice_done, S + 32)
            for c in range(2):
                sp.dma_start(yt[2][:, :, c * W:(c + 1) * W], y_rows[(NT - 1) * P * TOPK:NT * P * TOPK, c * W:(c + 1) * W
                                                                    ].rearrange("(p k) d -> p k d", k=TOPK)).then_inc(y_last[c], 16)
            for t in range(NT):
                sp.wait_ge(out_left, t + 1)
                sp.wait_ge(out_right, t + 1)
                sp.dma_start(out[t * P:(t + 1) * P, :], xres[:, t, :]).then_inc(out_stored, 16)
            sp.wait_ge(out_stored, 16 * NT)

        @block.gpsimd
        def _(pool):
            step = Count(pool, pool_step)
            step.inc(nc.gpsimd.memset(ident[:, :], 0.0))
            step.inc(nc.gpsimd.memset(intra[:, :], 1.0))
            step.inc(nc.gpsimd.memset(sel[:, :, :], 0.0))
            step.inc(nc.gpsimd.memset(r_one[:, :], 1.0))
            step.inc(nc.gpsimd.memset(r_neg[:, :], 0.0))
            step.link(nc.gpsimd.memset(wg_raw[:, :, :], 0.0))
            for n, c in enumerate((C_I, C_F)):
                pool.dma_start(wg_raw[:, :, 32 * n:32 * n + MH],
                               A["w_in"][:, c:c + MH].rearrange("(k p) n -> p k n", p=P)).then_inc(gate_w_landed, 16)
            step.inc(nc.gpsimd.affine_select(out=ident[:, :], in_=ident[:, :], compare_op=ALU.not_equal, fill=1.0,
                                             base=0, pattern=[[-1, P]], channel_multiplier=1))
            step.inc(nc.gpsimd.affine_select(out=intra[:, :], in_=intra[:, :], compare_op=ALU.is_ge, fill=0.0,
                                             base=0, pattern=[[1, P]], channel_multiplier=-1))
            step.inc(nc.gpsimd.affine_select(out=sel[:, :, :], in_=sel[:, :, :], compare_op=ALU.not_equal, fill=1.0,
                                             base=0, pattern=[[-1, MH], [0, P]], channel_multiplier=1))
            step.inc(nc.gpsimd.memset(r_one[:, :].rearrange("p (c l) -> p c l", l=CHUNK)[:, :, 0:1], 0.0))
            step.link(nc.gpsimd.memset(r_neg[:, :].rearrange("p (c l) -> p c l", l=CHUNK)[:, :, 0:1], BIG_NEG))
            nc.gpsimd.memset(intra[0:CHUNK, CHUNK:P], 0.0).then_inc(const_ready, 1)
            nc.gpsimd.memset(ones[:, :], 1.0).then_inc(const_ready, 1)
            nc.gpsimd.memset(q_pad[:, :, :, :], 0.0).then_inc(const_ready, 1)
            nc.gpsimd.memset(m_row[:, 0:1], 0.0).then_inc(const_ready, 1)
            nc.gpsimd.memset(eps_ln[:, :], LN_EPS).then_inc(const_ready, 1)
            nc.gpsimd.memset(eps_rms[:, :], RMS_EPS).then_inc(const_ready, 1)
            nc.gpsimd.memset(vme[:, :, :, MV:MVE], 1.0).then_inc(const_ready, 1)
            pool.wait_ge(gates_done, 1)
            nc.gpsimd.memset(state[:, 0, :], 0.0).then_inc(const_ready, 1)
            for h in range(MH):
                pool.wait_ge(wexp_ready, h + 1)
                nc.gpsimd.tensor_tensor(wexp[:, :, :], wexp[:, :, :],
                                        intra[:, :].unsqueeze(1).to_broadcast([P, NT, P]),
                                        ALU.mult).then_inc(wmask_ready, 1)
                if h == 1:
                    pool.wait_ge(drained, drains("u"))
                    for g in range(GG):
                        pool.wait_ge(mixed_read, g + 1)
                        part = uT[:, g, :].rearrange("p (t c) -> p t c", t=NT)
                        nc.gpsimd.tensor_tensor(part, part, v_sb[:, :, g * P:(g + 1) * P], ALU.mult).then_inc(a_ready, 1)
            pool.wait_ge(wmask_ready, MH)
            pool.wait_ge(ml_ready, NK)
            pool.wait_ge(y_ready, 8)
            step.inc(nc.gpsimd.memset(before[:, :], 1.0))
            step.inc(nc.gpsimd.memset(pos[:, :, :], -1.0))
            step.link(nc.gpsimd.memset(table[:, :, :, :], 0.0))
            nc.gpsimd.affine_select(out=before[:, :], in_=before[:, :], compare_op=ALU.is_gt, fill=0.0, base=0,
                                    pattern=[[1, P]], channel_multiplier=-1).then_inc(route_const, 1)
            for dst, pattern, base, cm in ((slot_no, [[1, P]], 0, 0), (iota8, [[1, 8]], 0, 0),
                                           (in_tile, [[0, 1]], 0, 1), (tile_no, [[1, NT]], -NOWHERE, 0)):
                nc.gpsimd.iota(dst[:, :], pattern=pattern, base=base, channel_multiplier=cm,
                               allow_small_or_imprecise_dtypes=True).then_inc(route_const, 1)
            def gain_and_offset(t, centred_sem, last_sem):
                pool.wait_ge(centred_sem, t + 1)
                step.link(nc.gpsimd.tensor_tensor(xres[:, t, W:D], xres[:, t, W:D], bias_bc[1][:, W:D], ALU.mult))
                nc.gpsimd.tensor_tensor(xres[:, t, W:D], xres[:, t, W:D], bias_bc[0][:, W:D], ALU.add).then_inc(last_sem, 1)

            pool.wait_ge(bias_landed[3], 16)
            pool.wait_ge(bias_landed[4], 16)
            for t in range(NT):
                gain_and_offset(t, centred2, x1_right)
            pool.wait_ge(slice_done, 8 * NCHUNK)
            step.inc(nc.gpsimd.memset(xg[0][:, :], 0.0))
            step.link(nc.gpsimd.memset(xg[1][:, :], 0.0))

            pool.wait_ge(lo_ready, G + 1)
            for n in range(1, 3):
                pool.wait_ge(hi_ready, G + n + 1)
                nc.gpsimd.tensor_tensor(w_l[n % 2][:, :, :], raw[n % 2][:, :, :], w_h[n % 2][:, :, :].bitcast(F32),
                                        ALU.subtract).then_inc(lo_ready, 1)

            def gated_embedding(c, product):
                for t in range(NT):
                    pool.wait_ge(pg_ready, 4 * c + t + 1)
                    nc.gpsimd.tensor_tensor(sgp[c][:, t, :], sgp[c][:, t, :], product[:, t, :], ALU.mult).then_inc(gated, 1)

            def wait_for(*waits):
                values = [pool.to_reg(value) for _, value in waits]
                pool.wait_ge(x1_stored, 16 * NT)
                for (s, _), value in zip(waits, values):
                    pool.wait_ge(s, value)

            last_token, last_row = pool.to_reg(SEQ - 1), pool.to_reg(SEQ * TOPK - 1)

            def gather(n, q):
                pool.indirect_dma_start(xg[n][:, :], None, x1_rows, bass.IndirectOffsetOnAxis(ixg[q][:, 0:1], 0),
                                        bounds_check=last_token, oob_is_err=False).then_inc(gathered[n], 16)

            def rows_of_pass(ps_no, first=False):
                for n in range(2):
                    wait_for((list_ready, ps_no * NU + n + 1))
                    gather(n, n)
                if first:
                    gated_embedding(0, emb[0])

                def scatter(v, j):
                    wait_for((y_act, ps_no * NEXP + v + 1), (y_dve, ps_no * NEXP + v + 1))
                    pool.indirect_dma_start(y_rows, bass.IndirectOffsetOnAxis(ixs[j][:, 0:1], 0), y_sb[j % 2][:, :],
                                            None, bounds_check=last_row, oob_is_err=False).then_inc(scattered[j % 2], 16)

                def expert(u, j, r):
                    wait_for((list_ready, ps_no * NU + u + 3), (xgt_done, ps_no * (NEXP + 1) + u + 1))
                    gather(j % 2, (j + 2) % 4)
                    if j or not isinstance(u, int):
                        scatter(u - 1, (j - 1) % 4)

                experts_in_order(pool, expert, NEXP)
                scatter(NEXP - 1, 3)
                wait_for(*((gathered[n], (ps_no + 1) * (16 * NU // 2)) for n in range(2)),
                         *((scattered[n], (ps_no + 1) * (16 * NEXP // 2)) for n in range(2)),
                         (xgt_done, (ps_no + 1) * (NEXP + 1)))

            rows_of_pass(0, first=True)
            pool.wait_ge(load_ready, 1)
            with pool.If(pool.value_load(load_max[0:1, 0:1], min_val=0, max_val=SEQ) > P):
                with pool.Fori(1, NT) as ps_no:
                    rows_of_pass(ps_no)
            nc.gpsimd.memset(mark[:, 0:1], 0.0).then_inc(routed_done, 1)

            pool.wait_ge(emb_back, 16)
            gated_embedding(1, emb_again)

            def sum_rows(t, y, c0, c1):
                for n in (4, 2, 1):
                    step.link(nc.gpsimd.tensor_tensor(y[:, 0:n, c0:c1], y[:, 0:n, c0:c1], y[:, n:2 * n, c0:c1], ALU.add))
                if t == 0:
                    pool.wait_ge(wp_added, 2 * NT)
                nc.gpsimd.tensor_tensor(xres[:, t, c0:c1], xres[:, t, c0:c1], y[:, 0, c0:c1], ALU.add).then_inc(y_right, 1)

            for t in range(NT - 1):
                pool.wait_ge(y_landed[t % 2], 16 * (t // 2 + 1))
                sum_rows(t, yt[t % 2], YS, D)
            pool.wait_ge(ln2_landed, 32)
            for c in range(2):
                pool.wait_ge(y_last[c], 16)
                sum_rows(NT - 1, yt[2], c * W + YH, (c + 1) * W)
                gain_and_offset(c, centred3, out_right)
            for t in range(2, NT):
                gain_and_offset(t, centred3, out_right)

        @block.scalar
        def _(act):
            step = Count(act, act_step)

            def hi_split(s, landed, sliced=0):
                act.wait_ge(raw_landed[s], landed)
                wait_any(act, slice_done, sliced)
                nc.scalar.activation(w_h[s][:, :, :], raw[s][:, :, :], ACT.Copy).then_inc(hi_ready, 1)

            def split_ahead(c, between=None):
                hi_split(1, 16 * c + 16, 8 * c)
                if between:
                    between()
                hi_split(0, 16 * c + 32, 8 * c + 4)

            act.dma_start(bif[:, 0:1], A["b_in"][C_I:C_I + MH].unsqueeze(1)).then_inc(vec_landed, 16)
            act.dma_start(bif[:, 1:2], A["b_in"][C_F:C_F + MH].unsqueeze(1)).then_inc(vec_landed, 16)
            for n, (v, c) in enumerate([("b_in", C_Q), ("b_in", C_U), ("b_in", C_GA), ("b_in", C_GB),
                                        ("sg_ln_g", 0), ("sg_ln_b", 0), ("mh_g", 0)]):
                act.dma_start(vec[n * NK:(n + 1) * NK, :],
                              A[v][c:c + D].rearrange("(r c) -> r c", c=P)).then_inc(vec_landed, 16)
            act.dma_start(ws_in[:, :, :], A["w_s"].rearrange("g t s -> t g s")).then_inc(ws_landed, 16)
            act.dma_start(add_bc[:, :, :], A["b_s"].partition_broadcast(P)).then_inc(bs_landed, 16)
            act.dma_start(bias_bc[0][:, :], A["b_in"][C_VM:C_VM + D].partition_broadcast(P)).then_inc(bias_landed[0], 16)
            act.dma_start(bias_bc[1][:, :], A["b_in"][C_V:C_V + D].partition_broadcast(P)).then_inc(bias_landed[1], 16)

            for k in range(NK):
                act.wait_ge(xt_done, k + 1)
                nc.scalar.activation(xT_h[:, k, :], aux[:, k % 4, :], ACT.Copy).then_inc(xh_ready, 1)
            act.wait_ge(gate_w_landed, 32)
            nc.scalar.activation(wg_h[:, :, :], wg_raw[:, :, :], ACT.Copy).then_inc(gw_hi, 1)
            hi_split(0, 16)

            def gate_rows():
                act.wait_ge(vec_landed, 16 * 9)
                act.wait_ge(gates_done, 1)
                nc.scalar.activation(r_a[:, :], aux[0:MH, 0, :], ACT.Identity, bias=bif[:, 0:1]).then_inc(gates_read, 1)
                nc.scalar.activation(r_f[:, :], aux[32:32 + MH, 0, :], ACT.Identity,
                                     bias=bif[:, 1:2]).then_inc(gates_read, 1)
                act.wait_ge(gate_abs, 1)
                step.link(nc.scalar.activation(r_t[:, :], r_t[:, :], ACT.Exp, scale=-1.0))
                nc.scalar.activation(r_t[:, :], r_t[:, :], ACT.Ln, bias=ones[0:MH, 0:1]).then_inc(gate_log, 1)
                for n, (r, scale) in enumerate([(win_row, 1.0), (r_f, 1.0), (r_em, -1.0), (dec_row, 1.0)]):
                    act.wait_ge(exp_asked, n + 1)
                    nc.scalar.activation(r[:, :], r[:, :], ACT.Exp, scale=scale).then_inc(rows_ready, 1)

            def decay_matrix(h):
                act.wait_ge(arg_ready, h + 1)
                nc.scalar.activation(wexp[:, :, :], wexp[:, :, :], ACT.Exp).then_inc(wexp_ready, 1)

            def numerators(h):
                for t in range(NT):
                    act.wait_ge(num_den, NT * h + t + 1)
                    nc.scalar.activation(vme[:, t, h, 0:MV], aux[:, t, 0:MV], ACT.Copy)
                    act.wait_ge(num_read, NT * h + t)
                    nc.scalar.activation(junk[:, :], aux[:, t, 0:MV], ACT.Square,
                                         accum_out=ssq[:, t, h:h + 1]).then_inc(num_read, 1)

            for kind in KINDS:
                c0 = first_chunk[kind]
                if kind == "ga":
                    act.wait_ge(a_ready, GG)
                    for g in range(GG):
                        nc.scalar.activation(aT_h[:, g, :], uT[:, g, :], ACT.Copy).then_inc(ah_ready, 1)
                if kind == "o":
                    act.wait_ge(drained, drains("vm"))
                    act.dma_start(bias_bc[0][:, :], A["b_in"][C_O:C_O + D].partition_broadcast(P)).then_inc(
                        bias_landed[2], 16)
                    act.wait_ge(drained, drains("v"))
                    act.dma_start(bias_bc[1][:, :], A["ln1_g"].partition_broadcast(P)).then_inc(bias_landed[3], 16)

                if kind == "pb":
                    act.wait_ge(ml_ready, NK)
                    act.dma_start(p_in[:, :, :], A["p"].rearrange("(t p) n -> p t n", p=P)).then_inc(p_landed, 16)
                    act.dma_start(wr_raw[:, :, :], A["w_router"].rearrange("(k p) e -> p k e", p=P)).then_inc(wr_landed, 16)
                    act.dma_start(br_bc[:, :], A["b_router"].partition_broadcast(P)).then_inc(wr_landed, 16)

                def chunk(i, between=None, ahead=None):
                    c = c0 + i
                    split_ahead(c, between)
                    if ahead:
                        ahead()
                    if kind == "ga":
                        act.wait_ge(al_ready, GG)
                    for t in range(4):
                        if kind in ("qk", "u", "ga", "gb"):
                            act.wait_ge(slice_done, 8 * c + 5 + t)
                            dst, func, b = {"qk": (qkT, ACT.Identity, B_QK), "u": (uT, ACT.Gelu, B_U),
                                            "ga": (yT, ACT.Sigmoid, B_GA), "gb": (gbT, ACT.Sigmoid, B_GB)}[kind]
                            if kind == "qk":
                                to = qkT[:, bass.ds(i, 1), t, :].rearrange("p a n -> p (a n)")
                            else:
                                to = dst[:, bass.ds(4 * i + t, 1), :].rearrange("p a n -> p (a n)")
                            nc.scalar.activation(to, ps[:, t, :], func,
                                                 bias=bcol[:, bass.ds(b + 4 * i + t, 1)]).then_inc(drained, 1)
                        elif kind == "v":
                            act.wait_ge(drained, drains("v", i, t))
                            part = v_sb[:, t, bass.ds(i * W, W)]
                            nc.scalar.activation(part, part, ACT.Gelu).then_inc(v_ready, 1)
                        elif kind == "o":
                            act.wait_ge(drained, drains("o", i, t))
                            part = osig[:, t, bass.ds(i * W, W)]
                            nc.scalar.activation(part, part, ACT.Sigmoid).then_inc(o_ready, 1)
                        elif kind == "pb":
                            act.wait_ge(y_ready, 4 * i + t + 1)
                            part = yT[:, bass.ds(4 * i + t, 1), :]
                            nc.scalar.activation(yT_h[:, bass.ds(4 * i + t, 1), :], part, ACT.Copy).then_inc(yh_ready, 1)

                def norm_deviations():
                    decay_matrix(1)
                    act.wait_ge(var_ready, NT)
                    nc.scalar.activation(rstd[:, :], mv[:, :, 1:2].rearrange("p t o -> p (t o)"), ACT.Sqrt,
                                         bias=eps_ln[:, :]).then_inc(std_ready, 1)

                def mlstm_deviations():
                    act.wait_ge(ms_ready, 1)
                    nc.scalar.activation(hs2[:, :, :], hs2[:, :, :], ACT.Sqrt, bias=eps_rms[:, :]).then_inc(rms_ready, 1)
                    act.wait_ge(mb_ready, NT * MH)

                def mlstm_high(ks):
                    for k in ks:
                        act.wait_ge(mt_done, k + 1)
                        nc.scalar.activation(mT_h[:, k, :], aux[:, k % 4, :], ACT.Copy,
                                             scale=bcol[:, B_MG + k:B_MG + k + 1]).then_inc(mh_ready, 1)

                if kind == "qk":
                    chunk(0, between=gate_rows)
                    chunk(1)
                elif kind == "u":
                    chunk(0, between=norm_deviations)
                    chunk(1)
                elif kind == "gb":
                    chunk(0, between=mlstm_deviations)
                    mlstm_high(range(0, 4))
                    chunk(1, ahead=lambda: mlstm_high(range(4, NK)))
                    for t in range(NT):
                        act.dma_start(xres[:, t, :], A["x"][t * P:(t + 1) * P, :]).then_inc(xres_landed, 16)
                else:
                    with act.Fori(0, 2) as i:
                        chunk(i)

                if kind == "pb":
                    for k in range(2):
                        act.wait_ge(pt_done, k + 1)
                        nc.scalar.activation(pT_h[:, k, :], aux[:, k, :], ACT.Copy).then_inc(ph_ready, 1)
                if kind == "vm":
                    decay_matrix(0)
                if kind == "v":
                    numerators(0)
                if kind == "u":
                    numerators(1)
                    decay_matrix(2)
                if kind == "ga":
                    numerators(2)
                    decay_matrix(3)
                if kind == "pa":
                    numerators(3)
                if kind == "o":
                    act.wait_ge(drained, drains("o"))
                    act.dma_start(bias_bc[0][:, :], A["ln1_b"].partition_broadcast(P)).then_inc(bias_landed[4], 16)


            def deviation(t, mv_, rstd_, var_sem, std_sem):
                act.wait_ge(var_sem, t + 1)
                nc.scalar.activation(rstd_[:, t:t + 1], mv_[:, t, 1:2], ACT.Sqrt, bias=eps_ln[:, :]).then_inc(std_sem, 1)

            def centre(t, rstd_, off_, coef_sem, centred_sem):
                act.wait_ge(coef_sem, t + 1)
                nc.scalar.activation(xres[:, t, :], xres[:, t, :], ACT.Identity, scale=rstd_[:, t:t + 1],
                                     bias=off_[:, t:t + 1]).then_inc(centred_sem, 1)

            def embedding(n):
                act.wait_ge(slice_done, S + n + 1)
                nc.scalar.activation(emb[n // 4][:, n % 4, :], ps[:, 1 + n % 3, :], ACT.Copy).then_inc(wp_read, 1)

            def x1_high(t):
                for n in range(2):
                    act.wait_ge(x1t_done, 2 * t + n + 1)
                    nc.scalar.activation(x1T_h[:, n * HK:(n + 1) * HK, t * P:(t + 1) * P], tiles((2 * t + n) % 4),
                                         ACT.Copy).then_inc(x1h_ready, 1)

            for t in range(NT):
                deviation(t, mv2, rstd2, var2_ready, std2_ready)
                if t:
                    centre(t - 1, rstd2, off2, coef2_ready, centred2)
            embedding(0)
            centre(3, rstd2, off2, coef2_ready, centred2)
            embedding(1)
            embedding(2)
            x1_high(0)
            x1_high(1)
            hi_split(1, R + 16, S)
            for n in range(3, 6):
                embedding(n)
            x1_high(2)
            embedding(6)
            embedding(7)
            x1_high(3)
            act.wait_ge(wp_read, 8)
            act.dma_start(emb_rows.rearrange("(t p) n -> p t n", p=P), emb[1][:, :, :]).then_inc(emb_stored, 16)
            for t in range(NT):
                act.wait_ge(x1_left, t + 1)
                act.wait_ge(x1_right, t + 1)
                act.dma_start(x1_rows[t * P:(t + 1) * P, :], xres[:, t, :]).then_inc(x1_stored, 16)
            act.dma_start(bias_bc[0][:, :], A["b_pg"].partition_broadcast(P)).then_inc(bpg_landed, 16)
            act.dma_start(bias_bc[1][:, :], A["ln2_g"].partition_broadcast(P)).then_inc(ln2_landed, 16)
            act.wait_ge(router_done, NT)
            nc.scalar.activation(scores[:, :, :], ps[:, 0, 0:NT * NEXP].rearrange("p (t e) -> p t e", t=NT),
                                 ACT.Sigmoid).then_inc(scores_ready, 1)
            hi_split(0, R + 32, S + 8)

            def gate_sigmoid(c):
                for t in range(NT):
                    act.wait_ge(pg_read, 4 * c + t + 1)
                    nc.scalar.activation(sgp[c][:, t, :], sgp[c][:, t, :], ACT.Sigmoid).then_inc(pg_ready, 1)

            gate_sigmoid(0)

            def xgt_copy(n, count):
                act.wait_ge(xgt_done, count)
                nc.scalar.activation(xgT[n][:, 0:HK, :], ps[:, 0, :].rearrange("p (k s) -> p k s", k=HK),
                                     ACT.Copy).then_inc(xgt_act, 1)

            def experts_of_pass(ps_no):
                T0, E0, S0 = ps_no * (NEXP + 1), ps_no * NEXP, ps_no * (16 * NEXP // 2)

                def rows_out(v, n, scattered_before):
                    act.wait_ge(dn_done, E0 + v + 1)
                    wait_any(act, scattered[n], S0 + scattered_before)
                    nc.scalar.activation(y_sb[n][:, 0:W], aux[:, 2, :], ACT.Copy).then_inc(y_act, 1)

                def expert(u, j, r):
                    act.wait_ge(gu_done, E0 + u + 1)
                    nc.scalar.activation(sg[:, :], ps[:, 2, 0:DE], ACT.Silu).then_inc(silu_ready, 1)
                    xgt_copy((j + 1) % 2, T0 + u + 2)
                    if j or not isinstance(u, int):
                        rows_out(u - 1, (j - 1) % 2, 32 * r + 16 * ((j - 1) // 2))
                    act.wait_ge(hidt_done, E0 + u + 1)
                    nc.scalar.activation(hidT[:, :, :], aux[:, 0, 0:2 * P].rearrange("p (k s) -> p k s", k=2),
                                         ACT.Copy).then_inc(hidt_ready, 1)

                xgt_copy(0, T0 + 1)
                experts_in_order(act, expert, NEXP)
                rows_out(NEXP - 1, 1, 16 * (NEXP // 2 - 1))

            experts_of_pass(0)
            act.wait_ge(load_ready, 1)
            with act.If(act.value_load(load_max[0:1, 0:1], min_val=0, max_val=SEQ) > P):
                with act.Fori(1, NT) as ps_no:
                    experts_of_pass(ps_no)
            nc.scalar.activation(mark[:, 1:2], ones[:, 0:1], ACT.Copy).then_inc(experts_over, 1)

            act.wait_ge(experts_over, 2)
            hi_split(1, R + 32)
            hi_split(0, R + 48)
            hi_split(1, R + 64, S + 20)
            gate_sigmoid(1)
            act.dma_start(bias_bc[0][:, :], A["ln2_b"].partition_broadcast(P)).then_inc(ln2_landed, 16)
            hi_split(0, R + 80, S + 24)
            hi_split(1, R + 80, S + 28)
            for t in range(NT):
                act.wait_ge(slice_done, S + 28 + t + 1)
                nc.scalar.activation(sg_s[:, t, :], ps[:, t, 0:DE], ACT.Silu).then_inc(sh_silu, 1)
            for k in range(2):
                act.wait_ge(ht_done, k + 1)
                nc.scalar.activation(hsT_h[:, k, :], aux[:, k, :], ACT.Copy).then_inc(hh_ready, 1)
            for t in range(NT):
                deviation(t, mv3, rstd3, var3_ready, std3_ready)
                if t in (1, 2):
                    centre(t - 1, rstd3, off3, coef3_ready, centred3)
                if t == 2:
                    centre(2, rstd3, off3, coef3_ready, centred3)
            centre(3, rstd3, off3, coef3_ready, centred3)

        @block.vector
        def _(dve):
            step = Count(dve, dve_step)
            TT = nc.vector.tensor_tensor
            STT = nc.vector.scalar_tensor_tensor

            def lo_split(s, rounded):
                dve.wait_ge(hi_ready, rounded)
                TT(w_l[s][:, :, :], raw[s][:, :, :], w_h[s][:, :, :].bitcast(F32), ALU.subtract).then_inc(lo_ready, 1)

            for k in range(NK):
                dve.wait_ge(xh_ready, k + 1)
                TT(xT_l[:, k, :], aux[:, k % 4, :], xT_h[:, k, :].bitcast(F32), ALU.subtract).then_inc(xl_ready, 1)
            dve.wait_ge(gw_hi, 1)
            TT(wg_l[:, :, :], wg_raw[:, :, :], wg_h[:, :, :].bitcast(F32), ALU.subtract).then_inc(gw_lo, 1)
            dve.wait_ge(vec_done, 1)
            nc.vector.tensor_copy(bcol[:, :], aux[:, 1, 0:NROW]).then_inc(bcol_ready, 1)
            lo_split(0, 1)
            for n in range(2):
                dve.wait_ge(wst_done, n + 1)
                step.link(nc.vector.tensor_copy(wsT[:, 4 * n:4 * n + 4, :], tiles(2 + n)))
            nc.vector.memset(wsT[CHUNK:P, :, 0:CHUNK], 0.0).then_inc(wst_ready, 1)

            def gate_rows():
                blk = lambda r: r[:, :].rearrange("p (c l) -> p c l", l=CHUNK)
                last = lambda r: blk(r)[:, :, CHUNK - 1:CHUNK]
                prev = m_row[:, 0:NC].unsqueeze(2)
                dve.wait_ge(gates_read, 2)
                dve.wait_ge(const_ready, 7)
                STT(r_t[:, :], r_f[:, :], -1.0, r_f[:, :], ALU.mult, ALU.max).then_inc(gate_abs, 1)
                dve.wait_ge(gate_log, 1)
                step.link(STT(r_f[:, :], r_f[:, :], 0.0, r_t[:, :], ALU.min, ALU.subtract))
                step.link(nc.vector.tensor_tensor_scan(r_b[:, :], r_one[:, :], r_f[:, :], 0.0, ALU.mult, ALU.add))
                step.link(TT(r_a[:, :], r_a[:, :], r_b[:, :], ALU.subtract))
                step.link(nc.vector.tensor_tensor_scan(r_cm[:, :], r_neg[:, :], r_a[:, :], BIG_NEG, ALU.add, ALU.max))
                g3 = g_row[:, :].unsqueeze(2)
                step.link(TT(g3, last(r_b), last(r_cm), ALU.add))
                step.link(nc.vector.tensor_copy(dec_row[:, :].unsqueeze(2), last(r_b)))
                step.link(nc.vector.tensor_tensor_scan(m_row[:, 1:NC + 1], dec_row[:, :], g_row[:, :], 0.0,
                                                       ALU.add, ALU.max))
                step.link(TT(blk(u_row), blk(r_cm), prev.to_broadcast([MH, NC, CHUNK]), ALU.max))
                TT(blk(win_row), prev.to_broadcast([MH, NC, CHUNK]), blk(u_row), ALU.subtract).then_inc(exp_asked, 1)
                TT(blk(r_f), blk(r_a), last(u_row).to_broadcast([MH, NC, CHUNK]), ALU.subtract).then_inc(exp_asked, 1)
                TT(r_em[:, :], r_b[:, :], u_row[:, :], ALU.add).then_inc(exp_asked, 1)
                TT(dec_row[:, :].unsqueeze(2), prev, last(u_row), ALU.subtract).then_inc(exp_asked, 1)

            def deviation(t, stat_, mv_, var_sem):
                nc.vector.bn_aggr(mv_[:, t, :], stat_[:, t, :, :]).then_inc(var_sem, 1)

            def coefficients(t, mv_, rstd_, off_, std_sem, coef_sem):
                dve.wait_ge(std_sem, t + 1)
                r = rstd_[:, t:t + 1]
                step.link(nc.vector.reciprocal(r, r))
                STT(off_[:, t:t + 1], mv_[:, t, 0:1], -1.0, r, ALU.mult, ALU.mult).then_inc(coef_sem, 1)

            def gain_and_offset(t, centred_sem, last_sem):
                dve.wait_ge(centred_sem, t + 1)
                step.link(TT(xres[:, t, 0:W], xres[:, t, 0:W], bias_bc[1][:, 0:W], ALU.mult))
                TT(xres[:, t, 0:W], xres[:, t, 0:W], bias_bc[0][:, 0:W], ALU.add).then_inc(last_sem, 1)

            def token_columns():
                dve.wait_ge(cols_done, 2)
                nc.vector.tensor_copy(dec_bc[:, :, :], aux[:, 0, 0:MH * NC].rearrange("p (h c) -> p h c", h=MH)
                                      ).then_inc(cols_ready, 1)
                nc.vector.tensor_copy(cols[:, :, :], aux[:, 1, 0:NT * 3 * MH].rearrange(
                    "p (t c) -> p t c", t=NT)).then_inc(cols_ready, 1)
                dve.wait_ge(cols_ready, 2)
                dve.wait_ge(bs_landed, 16)
                dve.wait_ge(bcol_ready, 1)
                for g in range(GG):
                    dve.wait_ge(rsum_done, g // 4 + 1)
                    STT(add_bc[:, g, :], aux[:, 2 + g // 4, (g % 4) * P:(g % 4 + 1) * P],
                        bcol[:, B_SB + g:B_SB + g + 1], add_bc[:, g, :], ALU.mult, ALU.add).then_inc(rsum_read, 1)
                dve.wait_ge(rsum_read, GG)

            def head_inputs(h):
                full = [P, NT, P]
                a_col = over_free(cols[:, :, h:h + 1].rearrange("p t o -> p (t o)"), full)
                k_col = over_free(cols[:, :, MH + h:MH + h + 1].rearrange("p t o -> p (t o)"), full)
                dve.wait_ge(a_done, 4 * h + 4)
                if h:
                    dve.wait_ge(num_done, NT * h)
                step.link(TT(wexp[:, :, :], tiles(1), a_col, ALU.max))
                TT(wexp[:, :, :], a_col, wexp[:, :, :], ALU.subtract).then_inc(arg_ready, 1)
                TT(kw[:, :, :], tiles(3), k_col, ALU.mult).then_inc(head_ready, 1)
                dve.wait_ge(drained, drains("qk"))
                qT = qkT[:, 0, h, :].rearrange("p (t c l) -> p t c l", t=NT, l=CHUNK)
                win = aux[:, 2, :].rearrange("p (t c l) -> p t c l", t=NT, l=CHUNK)
                for c in range(2):
                    STT(q_pad[:, :, c, c * CHUNK:(c + 1) * CHUNK], qT[:, :, c, :], QK ** -0.5, win[:, :, c, :],
                        ALU.mult, ALU.mult).then_inc(head_ready, 1)
                dve.wait_ge(wmask_ready, h + 1)
                STT(wS[:, :, :], tiles(0), QK ** -0.5, wexp[:, :, :], ALU.mult, ALU.mult).then_inc(head_ready, 1)

            def head_states(h):
                dve.wait_ge(const_ready, 8)
                for c in range(NC - 1):
                    dve.wait_ge(kv_done, (NC - 1) * h + c + 1)
                    STT(state[:, c + 1, :], state[:, c, :], dec_bc[:, h, c:c + 1], aux[:, c % 4, 0:MVE],
                        ALU.mult, ALU.add).then_inc(state_ready, 1)
                    dve.wait_ge(state_ready, (NC - 1) * h + c + 1)

            def head_den(h):
                for t in range(NT):
                    dve.wait_ge(num_done, NT * h + t + 1)
                    d = den[:, t, h:h + 1]
                    step.link(TT(d, aux[:, t, MV:MVE], cols[:, t, 2 * MH + h:2 * MH + h + 1], ALU.max))
                    STT(d, aux[:, t, MV:MVE], -1.0, d, ALU.mult, ALU.max).then_inc(num_den, 1)

            for kind in KINDS:
                c0 = first_chunk[kind]
                if kind in ("vm", "v", "o"):
                    dve.wait_ge(bias_landed[{"vm": 0, "v": 1, "o": 2}[kind]], 16)
                if kind == "vm":
                    dve.wait_ge(const_ready, 7)
                if kind == "out":
                    dve.wait_ge(xres_landed, 16 * NT)
                if kind == "o":
                    dve.wait_ge(a_done, 16)

                def chunk(i, between=None, ahead=None):
                    c = c0 + i
                    lo_split(1, 2 * c + 2)
                    if between:
                        between()
                    lo_split(0, 2 * c + 3)
                    if ahead:
                        ahead()
                    for t in range(4):
                        if kind in ("vm", "v", "o", "pa", "pb", "out"):
                            dve.wait_ge(slice_done, 8 * c + 5 + t)
                        feat = bass.ds(4 * i + t, 1)
                        bank = ps[:, t, :]
                        if kind == "vm":
                            TT(vme[:, t, bass.ds(2 * i, 2), 0:MV], bank.rearrange("p (h v) -> p h v", v=MV),
                               bias_bc[0][:, bass.ds(i * W, W)].rearrange("p (h v) -> p h v", v=MV),
                               ALU.add).then_inc(drained, 1)
                        elif kind in ("v", "o"):
                            dst, b = {"v": (v_sb, 1), "o": (osig, 0)}[kind]
                            TT(dst[:, t, bass.ds(i * W, W)], bank, bias_bc[b][:, bass.ds(i * W, W)],
                               ALU.add).then_inc(drained, 1)
                        elif kind == "pa":
                            dve.wait_ge(drained, drains("ga"))
                            part = yT[:, feat, :].rearrange("p a n -> p (a n)")
                            TT(part, bank, part, ALU.mult).then_inc(drained, 1)
                        elif kind == "pb":
                            dve.wait_ge(drained, drains("gb"))
                            part = yT[:, feat, :].rearrange("p a n -> p (a n)")
                            TT(tmp[:, :], bank, gbT[:, feat, :].rearrange("p a n -> p (a n)"),
                               ALU.mult).then_inc(drained, 1)
                            dve.wait_ge(drained, drains(kind, i, t))
                            TT(part, part, tmp[:, :], ALU.add).then_inc(y_ready, 1)
                            dve.wait_ge(y_ready, 4 * i + t + 1)
                        elif kind == "out":
                            part = xres[:, t, i * W:(i + 1) * W]
                            STT(part, part, ALPHA, bank, ALU.mult, ALU.add).then_inc(drained, 1)
                            dve.wait_ge(drained, drains("out", i, t))
                            nc.vector.bn_stats(stat2[:, t, i, :], part).then_inc(stat2_ready, 1)
                            if i == 1:
                                dve.wait_ge(stat2_ready, NT + t + 1)
                                deviation(t, stat2, mv2, var2_ready)
                                if t >= 1:
                                    coefficients(t - 1, mv2, rstd2, off2, std2_ready, coef2_ready)
                                if t >= 2:
                                    gain_and_offset(t - 2, centred2, x1_left)
                    if kind == "pb":
                        for t in range(4):
                            dve.wait_ge(yh_ready, 4 * i + t + 1)
                            feat = bass.ds(4 * i + t, 1)
                            TT(yT_l[:, feat, :], yT[:, feat, :], yT_h[:, feat, :].bitcast(F32),
                               ALU.subtract).then_inc(yl_ready, 1)

                def norm_of_v():
                    head_inputs(1)
                    dve.wait_ge(v_ready, 8)
                    for t in range(NT):
                        for n in range(2):
                            step.inc(nc.vector.bn_stats(stat[:, t, n, :], v_sb[:, t, n * W:(n + 1) * W]))
                    dve.wait_ge(dve_step, step.base + step.more)
                    for t in range(NT):
                        nc.vector.bn_aggr(mv[:, t, :], stat[:, t, :, :]).then_inc(var_ready, 1)

                def centre_v():
                    dve.wait_ge(var_ready, NT)
                    dve.wait_ge(std_ready, 1)
                    step.link(nc.vector.reciprocal(rstd[:, :], rstd[:, :]))
                    for t in range(NT):
                        nc.vector.tensor_scalar(v_sb[:, t, :], v_sb[:, t, :], mv[:, t, 0:1], rstd[:, t:t + 1],
                                                ALU.subtract, ALU.mult).then_inc(vn_ready, 1)

                def mlstm_branch():
                    dve.wait_ge(num_read, NT * MH)
                    dve.wait_ge(num_den, NT * MH)
                    step.link(nc.vector.reciprocal(den[:, :, :], den[:, :, :]))
                    step.link(TT(hs2[:, :, :], den[:, :, :], den[:, :, :], ALU.mult))
                    STT(hs2[:, :, :], hs2[:, :, :], 1.0 / MV, ssq[:, :, :], ALU.mult, ALU.mult).then_inc(ms_ready, 1)
                    dve.wait_ge(rms_ready, 1)
                    step.link(nc.vector.reciprocal(hs2[:, :, :], hs2[:, :, :]))
                    step.link(TT(hsc[:, :, :], hs2[:, :, :], den[:, :, :], ALU.mult))
                    dve.wait_ge(o_ready, 8)
                    for t in range(NT):
                        for h in range(MH):
                            part = osig[:, t, h * MV:(h + 1) * MV]
                            STT(part, vme[:, t, h, 0:MV], hsc[:, t, h:h + 1], part, ALU.mult,
                                ALU.mult).then_inc(mb_ready, 1)

                def mlstm_low(ks):
                    for k in ks:
                        dve.wait_ge(mh_ready, k + 1)
                        STT(mT_l[:, k, :], aux[:, k % 4, :], bcol[:, B_MG + k:B_MG + k + 1],
                            mT_h[:, k, :].bitcast(F32), ALU.mult, ALU.subtract).then_inc(ml_ready, 1)

                if kind == "qk":
                    chunk(0, between=gate_rows)
                    chunk(1)
                elif kind == "u":
                    chunk(0, between=norm_of_v, ahead=centre_v)
                    chunk(1)
                elif kind == "gb":
                    chunk(0, between=mlstm_branch)
                    mlstm_low(range(0, 4))
                    chunk(1, ahead=lambda: mlstm_low(range(4, NK)))
                elif kind == "out":
                    dve.wait_ge(bias_landed[3], 16)
                    dve.wait_ge(bias_landed[4], 16)
                    chunk(0)
                    chunk(1)
                    gain_and_offset(2, centred2, x1_left)
                    coefficients(3, mv2, rstd2, off2, std2_ready, coef2_ready)
                    gain_and_offset(3, centred2, x1_left)
                else:
                    with dve.Fori(0, 2) as i:
                        chunk(i)

                if kind == "pb":
                    for k in range(2):
                        dve.wait_ge(ph_ready, k + 1)
                        TT(pT_l[:, k, :], aux[:, k, :], pT_h[:, k, :].bitcast(F32), ALU.subtract).then_inc(pl_ready, 1)
                if kind == "vm":
                    token_columns()
                    head_inputs(0)
                if kind == "v":
                    head_states(0)
                    head_den(0)
                if kind == "u":
                    for g in range(GG):
                        dve.wait_ge(mixed_done, g + 1)
                        STT(v_sb[:, :, g * P:(g + 1) * P], tiles(g % 4),
                            bcol[:, B_SG + g:B_SG + g + 1], add_bc[:, g, :].unsqueeze(1).to_broadcast([P, NT, P]),
                            ALU.mult, ALU.add).then_inc(mixed_read, 1)
                    head_states(1)
                    head_den(1)
                    head_inputs(2)
                    for g in range(GG):
                        dve.wait_ge(ah_ready, g + 1)
                        TT(aT_l[:, g, :], uT[:, g, :], aT_h[:, g, :].bitcast(F32), ALU.subtract).then_inc(al_ready, 1)
                if kind == "ga":
                    head_states(2)
                    head_den(2)
                    head_inputs(3)
                if kind == "pa":
                    head_states(3)
                    head_den(3)

            for t in range(NT):
                for n in range(2):
                    dve.wait_ge(x1h_ready, 2 * t + n + 1)
                    part = (slice(None), slice(n * HK, (n + 1) * HK), slice(t * P, (t + 1) * P))
                    TT(x1T_l[part], tiles((2 * t + n) % 4), x1T_h[part].bitcast(F32), ALU.subtract).then_inc(x1l_ready, 1)
            dve.wait_ge(route_const, 5)

            step.inc(nc.vector.tensor_copy(table[:, :, :, 0], in_tile[:, :].unsqueeze(2).to_broadcast([P, NT, NU])))
            step.inc(nc.vector.tensor_copy(table[:, :, :, 1], tile_no[:, :].unsqueeze(2).to_broadcast([P, NT, NU])))
            full = [P, NT, NEXP]
            dve.wait_ge(scores_ready, 1)
            sel = sel8[:, :, :, :].rearrange("p t g e -> p t (g e)")
            best = rtmp[:, :, :].rearrange("p t (g e) -> p t g e", g=NGRP)
            step.link(TT(sel, scores[:, :, :], br_bc[:, :].unsqueeze(1).to_broadcast(full), ALU.add))
            for t in range(NT):
                for g in range(NGRP):
                    step.inc(nc.vector.max(best[:, t, g, :], sel8[:, t, g, :]))
            dve.wait_ge(dve_step, step.base + step.more)
            step.link(TT(grp[:, :, :].unsqueeze(3), best[:, :, :, 0:1], best[:, :, :, 1:2], ALU.add))
            for t in range(NT):
                step.inc(nc.vector.max(gtop[:, t, :], grp[:, t, :]))
            dve.wait_ge(dve_step, step.base + step.more)
            for t in range(NT):
                step.inc(nc.vector.max_index(gidx[:, t, :], gtop[:, t, :], grp[:, t, :]))
            dve.wait_ge(dve_step, step.base + step.more)
            step.link(nc.vector.tensor_copy(gidf[:, :, :], gidx[:, :, :]))
            for n in range(TOPG):
                dst = gmask if n == 0 else geq
                step.link(TT(dst[:, :, :], iota8[:, :].unsqueeze(1).to_broadcast([P, NT, 8]),
                             gidf[:, :, n:n + 1].to_broadcast([P, NT, 8]), ALU.is_equal))
                if n:
                    step.link(TT(gmask[:, :, :], gmask[:, :, :], geq[:, :, :], ALU.add))
            step.link(TT(sel8[:, :, :, :], sel8[:, :, :, :], gmask[:, :, :].unsqueeze(3).to_broadcast([P, NT, NGRP, 8]),
                         ALU.mult))
            step.link(nc.vector.tensor_scalar(gmask[:, :, :], gmask[:, :, :], -BIG_NEG, BIG_NEG, ALU.mult, ALU.add))
            step.link(TT(sel8[:, :, :, :], sel8[:, :, :, :], gmask[:, :, :].unsqueeze(3).to_broadcast([P, NT, NGRP, 8]),
                         ALU.add))
            for t in range(NT):
                step.inc(nc.vector.max(etop[:, t, :], sel[:, t, :]))
            dve.wait_ge(dve_step, step.base + step.more)
            for t in range(NT):
                step.inc(nc.vector.match_replace(rtmp[:, t, :], etop[:, t, :], sel[:, t, :], 3 * BIG_NEG))
            dve.wait_ge(dve_step, step.base + step.more)
            TT(chosen[:, :, :], rtmp[:, :, :], sel, ALU.not_equal).then_inc(chosen_ready, 1)
            dve.wait_ge(chosen_ready, 1)
            step.link(TT(scores[:, :, :], scores[:, :, :], chosen[:, :, :], ALU.mult))
            step.link(nc.vector.tensor_reduce(wsum[:, :], scores[:, :, :], AX.X, ALU.add))
            step.link(nc.vector.reciprocal(wsum[:, :], wsum[:, :]))
            weight = scores[:, :, :]
            step.link(STT(weight, weight, ROUTE_SCALE, wsum[:, :].unsqueeze(2).to_broadcast(full), ALU.mult, ALU.mult))
            step.link(nc.vector.tensor_copy(table[:, :, 0:NEXP, 3], weight))
            step.link(TT(weight, weight, table[:, :, 0:NEXP, 3], ALU.subtract))
            step.link(nc.vector.tensor_copy(table[:, :, 0:NEXP, 4], weight))
            step.inc(TT(table[:, :, 0:NEXP, 5], weight, table[:, :, 0:NEXP, 4], ALU.subtract))
            for t in range(NT):
                step.inc(nc.vector.tensor_tensor_scan(rtmp[:, t, :], ones[:, 0:NEXP], chosen[:, t, :], 0.0, ALU.mult, ALU.add))
            dve.wait_ge(dve_step, step.base + step.more)
            step.inc(nc.vector.tensor_copy(table[:, :, 0:NEXP, 2], rtmp[:, :, :]))
            dve.wait_ge(pos_done, NT)
            step.link(STT(pos[:, :, 0:NEXP], aux[:, 2, 0:NT * NEXP].rearrange("p (t e) -> p t e", t=NT), 1.0,
                          chosen[:, :, :], ALU.add, ALU.mult))
            nc.vector.tensor_scalar(pos[:, :, 0:NEXP], pos[:, :, 0:NEXP], -1.0, None, ALU.add).then_inc(table_ready, 1)
            dve.wait_ge(table_ready, 1)
            dve.wait_ge(pos_done, NT + 1)
            step.link(nc.vector.tensor_reduce(cmax[:, :], aux[:, 3, 0:NEXP], AX.X, ALU.max))
            nc.vector.tensor_copy(load_max[:, :], cmax[:, :]).then_inc(load_ready, 1)
            dve.wait_ge(load_ready, 1)

            def onehot_of(n, e, count):
                wait_any(dve, list_done, count)
                TT(onehot[n][:, :, :], slot_no[:, :].unsqueeze(1).to_broadcast([P, NT, P]),
                   pos[:, :, bass.ds(e, 1)].to_broadcast([P, NT, P]), ALU.is_equal).then_inc(onehot_ready, 1)

            def list_of(q, count):
                dve.wait_ge(list_done, count)
                wait_any(dve, rows_listed, count - 1)
                at = 8 * (q % 2)
                nc.vector.tensor_copy(list_parts[:, :], aux[:, 1, at:at + NLIST]).then_inc(list_step, 1)
                part = [list_parts[:, n:n + 1] for n in range(NLIST)]
                dve.wait_ge(list_step, 4 * count - 3)
                STT(list_token[:, :], part[1], float(P), part[0], ALU.mult, ALU.add).then_inc(list_step, 1)
                TT(list_weight[:, :], part[3], part[4], ALU.add).then_inc(list_step, 1)
                dve.wait_ge(list_step, 4 * count - 1)
                STT(list_row[:, :], list_token[:, :], float(TOPK), part[2], ALU.mult, ALU.add).then_inc(list_step, 1)
                nc.vector.tensor_scalar(ixg[q][:, :], list_token[:, :], float(P * NOWHERE), None, ALU.add)
                TT(cw[q][:, :], list_weight[:, :], part[5], ALU.add).then_inc(list_ready, 1)

            def rows_of(q, count):
                dve.wait_ge(list_step, 4 * count)
                nc.vector.tensor_scalar(ixs[q][:, :], list_row[:, :], float(P * NOWHERE * TOPK - 1), None,
                                        ALU.add).then_inc(rows_listed, 1)

            def xgt_copy(n, count):
                dve.wait_ge(xgt_done, count)
                nc.vector.tensor_copy(xgT[n][:, HK:NK, :], ps[:, 1, :].rearrange("p (k s) -> p k s", k=HK)).then_inc(xgt_dve, 1)

            def gate_read(c):
                dve.wait_ge(bpg_landed, 16)
                for t in range(NT):
                    dve.wait_ge(slice_done, S + 12 + 8 * c + t + 1)
                    TT(sgp[c][:, t, :], ps[:, t, :], bias_bc[0][:, c * W:(c + 1) * W], ALU.add).then_inc(pg_read, 1)

            def add_embedding(c):
                for t in range(NT):
                    part = (slice(None), t, slice(c * W, (c + 1) * W))
                    dve.wait_ge(gated, 4 * c + t + 1)
                    STT(xres[part], xres[part], ALPHA, sgp[c][:, t, :], ALU.mult, ALU.add).then_inc(wp_added, 1)

            def experts_of_pass(ps_no, again=False):
                T0, E0, L0 = ps_no * (NEXP + 1), ps_no * NEXP, ps_no * NU
                for n in range(2):
                    onehot_of(n, n, L0)
                for n in range(2):
                    if again:
                        dve.wait_ge(gathered[n], ps_no * (16 * NU // 2))
                        dve.wait_ge(scattered[0], ps_no * (16 * NEXP // 2))
                        dve.wait_ge(scattered[1], ps_no * (16 * NEXP // 2))
                    list_of(n, L0 + n + 1)
                    rows_of(n, L0 + n + 1)
                if not again:
                    gate_read(0)
                xgt_copy(0, T0 + 1)
                if not again:
                    dve.wait_ge(x1_stored, 16 * NT)
                    add_embedding(0)
                S0 = ps_no * (16 * NEXP // 2)

                def rows_out(v, n, scattered_before):
                    dve.wait_ge(dn_done, E0 + v + 1)
                    wait_any(dve, scattered[n], S0 + scattered_before)
                    nc.vector.tensor_copy(y_sb[n][:, W:2 * W], aux[:, 3, :]).then_inc(y_dve, 1)

                def expert(u, j, r):
                    onehot_of(j % 2, u + 2, L0 + u + 1)
                    dve.wait_ge(gu_done, E0 + u + 1)
                    dve.wait_ge(silu_ready, E0 + u + 1)
                    dve.wait_ge(list_ready, L0 + u + 1)
                    STT(hid[:, :], ps[:, 2, DE:2 * DE], cw[j][:, :], sg[:, :], ALU.mult, ALU.mult).then_inc(hid_ready, 1)
                    list_of((j + 2) % 4, L0 + u + 3)
                    xgt_copy((j + 1) % 2, T0 + u + 2)
                    if j or not isinstance(u, int):
                        rows_out(u - 1, (j - 1) % 2, 32 * r + 16 * ((j - 1) // 2))
                    wait_any(dve, scattered[j % 2], S0 + 32 * r + 16 * (j // 2))
                    rows_of((j + 2) % 4, L0 + u + 3)

                experts_in_order(dve, expert, NEXP)
                rows_out(NEXP - 1, 1, 16 * (NEXP // 2 - 1))

            def next_slots(ps_no):
                dve.wait_ge(onehot_ready, ps_no * NU)
                dve.wait_ge(list_done, ps_no * NU)
                nc.vector.tensor_scalar(slot_no[:, :], slot_no[:, :], float(P), None, ALU.add).then_inc(slots_moved, 1)
                dve.wait_ge(slots_moved, ps_no)

            experts_of_pass(0)
            with dve.If(dve.value_load(load_max[0:1, 0:1], min_val=0, max_val=SEQ) > P):
                with dve.Fori(1, NT) as ps_no:
                    next_slots(ps_no)
                    experts_of_pass(ps_no, again=True)
            nc.vector.memset(mark[:, 2:3], 0.0).then_inc(experts_over, 1)

            def lo_tail(n):
                s = n % 2
                dve.wait_ge(hi_ready, G + n + 1)
                TT(w_l[s][:, :, :], raw[s][:, :, :], w_h[s][:, :, :].bitcast(F32), ALU.subtract).then_inc(lo_ready, 1)

            lo_tail(3)
            lo_tail(4)
            lo_tail(5)
            dve.wait_ge(routed_done, 1)
            gate_read(1)
            lo_tail(6)

            def sum_rows(t, y, c0, c1):
                for n in (4, 2, 1):
                    step.link(TT(y[:, 0:n, c0:c1], y[:, 0:n, c0:c1], y[:, n:2 * n, c0:c1], ALU.add))
                TT(xres[:, t, c0:c1], xres[:, t, c0:c1], y[:, 0, c0:c1], ALU.add).then_inc(y_left, 1)

            def sum_tile(t):
                dve.wait_ge(y_landed[t % 2], 16 * (t // 2 + 1))
                sum_rows(t, yt[t % 2], 0, YS)

            add_embedding(1)
            dve.wait_ge(wp_added, 2 * NT)
            sum_tile(0)
            lo_tail(7)
            sum_tile(1)
            for t in range(NT):
                dve.wait_ge(sh_silu, t + 1)
                TT(hs[:, t, :], ps[:, t, DE:2 * DE], sg_s[:, t, :], ALU.mult).then_inc(sh_ready, 1)
            for k in range(2):
                dve.wait_ge(hh_ready, k + 1)
                TT(hsT_l[:, k, :], aux[:, k, :], hsT_h[:, k, :].bitcast(F32), ALU.subtract).then_inc(hl_ready, 1)
            sum_tile(2)
            dve.wait_ge(ln2_landed, 32)

            def add_shared(t, c):
                cols_ = slice(c * W, (c + 1) * W)
                TT(xres[:, t, cols_], xres[:, t, cols_], (aux if t < 2 else ps)[:, (2 * t + c) % 4, :],
                   ALU.add).then_inc(ds_added, 1)
                dve.wait_ge(ds_added, 2 * t + c + 1)
                step.inc(nc.vector.bn_stats(stat3[:, t, c, :], xres[:, t, cols_]))

            def last_half(c):
                dve.wait_ge(y_last[c], 16)
                sum_rows(NT - 1, yt[2], c * W, c * W + YH)

            def ffn_sum(t, sums):
                dve.wait_ge(slice_done, S + 32 + t + 1)
                dve.wait_ge(y_left, sums)
                dve.wait_ge(y_right, sums)
                for c in range(2):
                    add_shared(t, c)
                dve.wait_ge(dve_step, step.base + step.more)
                deviation(t, stat3, mv3, var3_ready)

            def coefficients3(t):
                coefficients(t, mv3, rstd3, off3, std3_ready, coef3_ready)

            ffn_sum(0, 1)
            ffn_sum(1, 2)
            coefficients3(0)
            last_half(0)
            ffn_sum(2, 3)
            coefficients3(1)
            gain_and_offset(0, centred3, out_left)
            last_half(1)
            coefficients3(2)
            gain_and_offset(1, centred3, out_left)
            ffn_sum(3, 5)
            gain_and_offset(2, centred3, out_left)
            coefficients3(3)
            gain_and_offset(3, centred3, out_left)

        @block.tensor
        def _(pe):
            mm = nc.tensor.matmul

            def product(bank, halves, k, t, first, last):
                (a_h, a_l), (b_h, b_l) = halves
                mm(bank, a_h, b_h, start=first, stop=False)
                mm(bank, a_h, b_l, start=False, stop=False)
                return mm(bank, a_l, b_h, start=False, stop=last)

            pe.wait_ge(const_ready, 7)
            for k in range(NK):
                if k >= 4:
                    pe.wait_ge(xl_ready, k - 3)
                for t in range(NT):
                    if k == 0:
                        pe.wait_ge(x_landed[t], 16)
                    ins = nc.tensor.transpose(aux[:, k % 4, t * P:(t + 1) * P], x_in[:, t, k * P:(k + 1) * P], ident[:, :])
                ins.then_inc(xt_done, 1)
            pe.wait_ge(vec_landed, 16 * 9)
            pe.wait_ge(xl_ready, 8)
            nc.tensor.transpose(aux[:, 1, 0:NROW], vec[:, :], ident[0:NROW, 0:NROW]).then_inc(vec_done, 1)
            pe.wait_ge(gw_lo, 1)
            for k in range(NK):
                ins = product(aux[:, 0, :], ((wg_h[:, k, :], wg_l[:, k, :]), (xT_h[:, k, :], xT_l[:, k, :])), k, 0,
                              k == 0, k == NK - 1)
            ins.then_inc(gates_done, 1)
            pe.wait_ge(ws_landed, 16)
            for g in range(GG):
                ins = nc.tensor.transpose(aux[:, 2 + g // 4, (g % 4) * P:(g % 4 + 1) * P], ws_in[:, g, :], ident[:, :])
                if g % 4 == 3:
                    ins.then_inc(wst_done, 1)

            def token_columns():
                pe.wait_ge(rows_ready, 4)
                pe.wait_ge(wst_ready, 1)
                pe.wait_ge(bcol_ready, 1)
                for h in range(MH):
                    ins = mm(aux[:, 0, h * NC:(h + 1) * NC], sel[:, h, :], dec_row[:, :], start=True, stop=True)
                ins.then_inc(cols_done, 1)
                for t in range(NT):
                    for n, r in enumerate((r_a, r_f, r_em)):
                        at = t * 3 * MH + n * MH
                        ins = nc.tensor.transpose(aux[:, 1, at:at + MH], r[:, t * P:(t + 1) * P], ident[0:MH, 0:MH])
                ins.then_inc(cols_done, 1)
                for g in range(2):
                    mm(aux[:, 2 + g, :], ones[:, :], wsT[:, 4 * g:4 * g + 4, :].rearrange("p g t -> p (g t)"),
                       start=True, stop=True).then_inc(rsum_done, 1)

            def head_inputs(h):
                kT, qT = qkT[:, 1, h, :], qkT[:, 0, h, :]
                if h == 0:
                    pe.wait_ge(drained, drains("qk"))
                    pe.wait_ge(cols_ready, 2)
                    pe.wait_ge(rsum_read, GG)
                else:
                    pe.wait_ge(num_read, NT * h)
                for t in range(NT):
                    at = slice(t * P, (t + 1) * P)
                    ins = mm(aux[:, 0, at], kT[:, at], qT[:, at], start=True, stop=True)
                ins.then_inc(a_done, 1)
                mm(aux[:, 1, :], sel[:, h, :], u_row[:, :], start=True, stop=True).then_inc(a_done, 1)
                mm(aux[:, 2, :], sel[:, h, :], win_row[:, :], start=True, stop=True).then_inc(a_done, 1)
                for t in range(NT):
                    at = slice(t * P, (t + 1) * P)
                    ins = nc.tensor.transpose(aux[:, 3, at], kT[:, at], ident[:, :])
                ins.then_inc(a_done, 1)

            def head_products(h):
                pe.wait_ge(head_ready, 4 * h + 4)
                pe.wait_ge(drained, drains("vm"))
                for c in range(NC - 1):
                    if c >= 4:
                        pe.wait_ge(state_ready, (NC - 1) * h + c - 3)
                    t, at = c // 2, slice((c % 2) * CHUNK, (c % 2 + 1) * CHUNK)
                    mm(aux[:, c % 4, 0:MVE], kw[at, t, :], vme[at, t, h, :], start=True, stop=True).then_inc(kv_done, 1)
                for t in range(NT):
                    pe.wait_ge(state_ready, (NC - 1) * h + (5, 6, 7, 7)[t])
                    bank = aux[:, t, 0:MVE]
                    mm(bank, wS[:, t, :], vme[:, t, h, :], start=True, stop=False)
                    mm(bank, q_pad[:, t, 0, :], state[:, 2 * t, :], start=False, stop=False)
                    mm(bank, q_pad[:, t, 1, :], state[:, 2 * t + 1, :], start=False, stop=True).then_inc(num_done, 1)

            moving = {"pa": (aT_h, aT_l), "pb": (mT_h, mT_l), "out": (yT_h, yT_l)}
            for n, kind in enumerate(KINDS):
                c0 = first_chunk[kind]
                m_h, m_l = moving.get(kind, (xT_h, xT_l))
                if kind == "pa":
                    pe.wait_ge(al_ready, GG)
                if kind == "pb":
                    pe.wait_ge(ml_ready, NK)
                if kind == "out":
                    pe.wait_ge(yl_ready, NK)

                def chunk(i, within=None):
                    for s in range(2):
                        if s == 1 and within:
                            within()
                        pe.wait_ge(lo_ready, 2 * (c0 + i) + s + 1)
                        for t in range(4):
                            if s == 0 and not (kind == KINDS[0] and isinstance(i, int) and i == 0):
                                pe.wait_ge(drained, 4 * (c0 + i) - 3 + t)
                            for kk in range(HK):
                                k = s * HK + kk
                                at = slice(t * P, (t + 1) * P)
                                if kind in FEATURE:
                                    halves = ((w_h[s][:, kk, at], w_l[s][:, kk, at]), (m_h[:, k, :], m_l[:, k, :]))
                                else:
                                    halves = ((m_h[:, k, at], m_l[:, k, at]), (w_h[s][:, kk, :], w_l[s][:, kk, :]))
                                ins = product(ps[:, t, :], halves, k, t, k == 0, k == NK - 1)
                            ins.then_inc(slice_done, 1)

                def mlstm_transposed(ks):
                    pe.wait_ge(mb_ready, NT * MH)
                    pe.wait_ge(num_read, NT * MH)
                    for k in ks:
                        if k >= 4:
                            pe.wait_ge(ml_ready, k - 3)
                        for t in range(NT):
                            ins = nc.tensor.transpose(aux[:, k % 4, t * P:(t + 1) * P], osig[:, t, k * P:(k + 1) * P],
                                                      ident[:, :])
                        ins.then_inc(mt_done, 1)

                if kind == KINDS[0]:
                    chunk(0)
                    chunk(1)
                elif kind == "gb":
                    chunk(0)
                    mlstm_transposed(range(0, 4))
                    chunk(1, within=lambda: mlstm_transposed(range(4, NK)))
                else:
                    with pe.Fori(0, 2) as i:
                        chunk(i)
                if kind == "vm":
                    token_columns()
                    head_inputs(0)
                if kind == "v":
                    head_products(0)
                    head_inputs(1)
                if kind == "u":
                    pe.wait_ge(vn_ready, NT)
                    pe.wait_ge(head_ready, 8)
                    for g in range(GG):
                        if g >= 4:
                            pe.wait_ge(mixed_read, g - 3)
                        for t in range(NT):
                            ins = mm(aux[:, g % 4, t * P:(t + 1) * P], v_sb[:, t, g * P:(g + 1) * P], wsT[:, g, :],
                                     start=True, stop=True)
                        ins.then_inc(mixed_done, 1)
                    pe.wait_ge(mixed_read, GG)
                    head_products(1)
                    head_inputs(2)
                if kind == "ga":
                    head_products(2)
                    head_inputs(3)
                if kind == "pa":
                    head_products(3)
                if kind == "pb":
                    pe.wait_ge(p_landed, 16)
                    for k in range(2):
                        for t in range(NT):
                            ins = nc.tensor.transpose(aux[:, k, t * P:(t + 1) * P], p_in[:, t, k * P:(k + 1) * P], ident[:, :])
                        ins.then_inc(pt_done, 1)


            def transpose_x1(t):
                for n in range(2):
                    pe.wait_ge((x1_left, x1_right)[n], t + 1)
                    b = 2 * t + n
                    if b >= 4:
                        pe.wait_ge(x1l_ready, b - 3)
                    for kk in range(HK):
                        k = n * HK + kk
                        ins = nc.tensor.transpose(aux[:, b % 4, kk * P:(kk + 1) * P], xres[:, t, k * P:(k + 1) * P],
                                                  ident[:, :])
                    ins.then_inc(x1t_done, 1)

            def route(t):
                pe.wait_ge(x1l_ready, 2 * t + 2)
                at = slice(t * P, (t + 1) * P)
                for k in range(NK):
                    for n, part in enumerate((x1T_h, x1T_l)):
                        ins = mm(ps[:, 0, t * NEXP:(t + 1) * NEXP], part[:, k, at].bitcast(F32), wr_raw[:, k, :],
                                 start=(k == 0 and n == 0), stop=(k == NK - 1 and n == 1))
                ins.then_inc(router_done, 1)

            def wide_rows(w, g):
                return w[g % 2][:, :, :].rearrange("p (k a) n -> p k (a n)", k=2)

            def short(bank, g, f_h, f_l, t, c):
                at, cols_ = slice(t * P, (t + 1) * P), slice(c * W, (c + 1) * W)
                for k in range(2):
                    ins = product(bank, ((f_h[:, k, at], f_l[:, k, at]), (wide_rows(w_h, g)[:, k, cols_],
                                                                          wide_rows(w_l, g)[:, k, cols_])), k, t, k == 0, k == 1)
                return ins

            def embedding(n):
                if n < 3:
                    pe.wait_ge(drained, drains("out", 1, 1 + n))
                else:
                    pe.wait_ge(wp_read, n - 2)
                short(ps[:, 1 + n % 3, :], 0, pT_h, pT_l, n % 4, n // 4).then_inc(slice_done, 1)

            def whole(g, s, tiles_=range(NT)):
                pe.wait_ge(lo_ready, G + g + 1)
                for t in tiles_:
                    at = slice(t * P, (t + 1) * P)
                    for kk in range(HK):
                        k = s * HK + kk
                        ins = product(ps[:, t, :], ((x1T_h[:, k, at], x1T_l[:, k, at]),
                                                    (w_h[g % 2][:, kk, :], w_l[g % 2][:, kk, :])), k, t, k == 0, k == NK - 1)
                    ins.then_inc(slice_done, 1)

            pe.wait_ge(pl_ready, 2)
            pe.wait_ge(lo_ready, G + 1)
            for n in range(3):
                embedding(n)
            transpose_x1(0)
            transpose_x1(1)
            for n in range(3, 6):
                embedding(n)
            pe.wait_ge(wr_landed, 32)
            pe.wait_ge(drained, drains("out", 1, 0))
            transpose_x1(2)
            route(0)
            embedding(6)
            embedding(7)
            transpose_x1(3)
            for t in range(1, NT):
                route(t)
            pe.wait_ge(scores_ready, 1)
            pe.wait_ge(wp_read, 8)
            whole(1, 0)
            pe.wait_ge(chosen_ready, 1)
            pe.wait_ge(route_const, 1)
            for t in range(NT):
                bank = aux[:, 2, t * NEXP:(t + 1) * NEXP]
                for s in range(t):
                    mm(bank, ones[:, :], chosen[:, s, :], start=(s == 0), stop=False)
                mm(bank, before[:, :], chosen[:, t, :], start=(t == 0), stop=True).then_inc(pos_done, 1)
            for t in range(NT):
                ins = mm(aux[:, 3, 0:NEXP], ones[:, :], chosen[:, t, :], start=(t == 0), stop=(t == NT - 1))
            ins.then_inc(pos_done, 1)

            def list_of(n, e, count):
                pe.wait_ge(onehot_ready, count)
                at = 8 * (n % 2)
                for t in range(NT):
                    ins = mm(aux[:, 1, at:at + NLIST], onehot[n % 2][:, t, :],
                             table[:, t, bass.ds(e, 1), :].rearrange("p e c -> p (e c)"), start=(t == 0), stop=(t == NT - 1))
                ins.then_inc(list_done, 1)

            def transposes(n, landed):
                pe.wait_ge(gathered[n], landed)
                for k in range(NK):
                    ins = nc.tensor.transpose(ps[:, k // HK, (k % HK) * P:(k % HK + 1) * P], xg[n][:, k:D:NK], ident[:, :])
                ins.then_inc(xgt_done, 1)

            def experts_of_pass(ps_no, first=False):
                T0, E0, L0 = ps_no * (NEXP + 1), ps_no * NEXP, ps_no * NU
                R0, W0 = ps_no * (16 * NU // 2), ps_no * (NEXP // 4)
                if first:
                    whole(2, 1, range(0, 2))
                    pe.wait_ge(table_ready, 1)
                list_of(0, 0, L0 + 1)
                if first:
                    whole(2, 1, range(2, 3))
                pe.wait_ge(list_ready, L0 + 1)
                list_of(1, 1, L0 + 2)
                if first:
                    whole(2, 1, range(3, 4))
                    pe.wait_ge(pg_read, NT)
                transposes(0, R0 + 16)

                def down(v, j, r):
                    pe.wait_ge(hidt_ready, E0 + v + 1)
                    pe.wait_ge(dn_landed[j], 16 * (W0 + r + 1))
                    wait_any(pe, y_act, E0 + v)
                    wait_any(pe, y_dve, E0 + v)
                    for c in range(2):
                        for k in range(2):
                            ins = mm(aux[:, 2 + c, :], hidT[:, k, :], dn[j][:, k, c * W:(c + 1) * W], start=(k == 0),
                                     stop=(k == 1))
                    ins.then_inc(dn_done, 1)

                def expert(u, j, r):
                    pe.wait_ge(xgt_act, T0 + u + 1)
                    pe.wait_ge(xgt_dve, T0 + u + 1)
                    pe.wait_ge(gu_landed[j], 32 * (W0 + r + 1))
                    for k in range(NK):
                        ins = mm(ps[:, 2, :], xgT[j % 2][:, k, :], gu[j][:, k, :], start=(k == 0), stop=(k == NK - 1))
                    ins.then_inc(gu_done, 1)
                    pe.wait_ge(list_ready, L0 + u + 2)
                    list_of(j, u + 2, L0 + u + 3)
                    transposes((j + 1) % 2, R0 + 32 * r + 16 * ((j + 1) // 2) + 16)
                    if j:
                        down(u - 1, j - 1, r)
                    elif not isinstance(u, int):
                        down(u - 1, 3, r - 1)
                    pe.wait_ge(hid_ready, E0 + u + 1)
                    for k in range(2):
                        ins = nc.tensor.transpose(aux[:, 0, k * P:(k + 1) * P], hid[:, k:DE:2], ident[:, :])
                    ins.then_inc(hidt_done, 1)

                experts_in_order(pe, expert, NEXP)
                down(NEXP - 1, 3, NEXP // 4 - 1)
                pe.wait_ge(y_act, E0 + NEXP)
                pe.wait_ge(y_dve, E0 + NEXP)
                pe.wait_ge(list_ready, L0 + NU)
                pe.wait_ge(xgt_act, T0 + NEXP + 1)
                pe.wait_ge(xgt_dve, T0 + NEXP + 1)

            experts_of_pass(0, first=True)
            pe.wait_ge(load_ready, 1)
            with pe.If(pe.value_load(load_max[0:1, 0:1], min_val=0, max_val=SEQ) > P):
                with pe.Fori(1, NT) as ps_no:
                    experts_of_pass(ps_no)

            whole(3, 0)
            whole(4, 1)
            pe.wait_ge(pg_read, 2 * NT)
            whole(5, 0)
            whole(6, 1)
            pe.wait_ge(sh_ready, NT)
            for k in range(2):
                for t in range(NT):
                    ins = nc.tensor.transpose(aux[:, k, t * P:(t + 1) * P], hs[:, t, k * P:(k + 1) * P], ident[:, :])
                ins.then_inc(ht_done, 1)
            pe.wait_ge(hl_ready, 2)
            pe.wait_ge(lo_ready, G + 8)
            for n in range(8):
                t, c = n // 2, n % 2
                ins = short((aux if n < 4 else ps)[:, n % 4, :], 7, hsT_h, hsT_l, t, c)
                if c == 1:
                    ins.then_inc(slice_done, 1)


IN_NAMES = ["x", "p", "w_in", "b_in", "sg_ln_g", "sg_ln_b", "w_s", "b_s", "mh_g", "w_pa", "w_pb", "w_out",
            "ln1_g", "ln1_b", "w_router", "b_router", "w_gate_e", "w_up_e", "w_down_e",
            "w_gate_s", "w_up_s", "w_down_s", "w_pg", "b_pg", "w_p", "ln2_g", "ln2_b"]


def kernel(**inputs):
    import numpy as _np
    import concourse.bacc as _bacc
    from concourse import mybir as _mybir
    from concourse.bass_utils import run_bass_kernel_spmd as _run

    nc = _bacc.Bacc("TRN2", target_bir_lowering=False, num_devices=1)
    arrays, aps = {}, {}
    for name in IN_NAMES:
        a = _np.ascontiguousarray(inputs[name])
        a = a[0]
        if name == "p":
            a = a[0]
        arrays[f"in_{name}"] = a
        aps[name] = nc.dram_tensor(f"in_{name}", a.shape, _mybir.dt.from_np(a.dtype), kind="ExternalInput").ap()
    out = nc.dram_tensor("out", (SEQ, D), _mybir.dt.float32, kind="ExternalOutput").ap()
    build(nc, aps, out)
    r = _run(nc, [arrays], core_ids=[0])
    return r.results[0]["out"].reshape(1, SEQ, D)
```
